# Optimizing a Trainium2 kernel written in Bass

```python
import jax, jax.numpy as jnp
from jax import lax
import numpy as np

D_MODEL = 1024
BATCH = 1
SEQ = 256
DEPTH = 2

N_EVEN = (DEPTH + 1) // 2
N_ODD = DEPTH // 2
D_FF = 2816
NORM_EPS = 1e-6
BLOCK = 128

A_HEADS = 8
A_HEAD_DIM = 64
A_BRANCHES = ((128, 1), (512, 4), (2048, 16))
B_HEADS = 8
B_NOPE_DIM = 64
B_ROPE_DIM = 32
B_V_DIM = 64
B_Q_RANK = 256
B_KV_RANK = 128
ROPE_THETA = 10000.0
A_QKV = 3 * A_HEADS * A_HEAD_DIM
AB_IN = A_QKV + B_Q_RANK + B_KV_RANK + B_ROPE_DIM
AB_OUT = A_HEADS * A_HEAD_DIM + B_HEADS * B_V_DIM
C_HEADS = 16
C_HEAD_DIM = 64
C_IN = 3 * C_HEADS * C_HEAD_DIM
C_OUT = C_HEADS * C_HEAD_DIM

kernel_name = 'hybrid_dilated_mla_stickbreak_macaron'

def rmsnorm(x, g):
    xf = x.astype(jnp.float32)
    y = xf * lax.rsqrt(jnp.mean(xf * xf, axis=-1, keepdims=True) + NORM_EPS)
    return (y * g.astype(jnp.float32)).astype(x.dtype)

def swiglu(x, w_gate, w_up, w_down):
    return (jax.nn.silu(x @ w_gate) * (x @ w_up)) @ w_down

def rope(x):
    s, dr = x.shape[1], x.shape[-1]
    inv = ROPE_THETA ** (-jnp.arange(0, dr, 2, dtype=jnp.float32) / dr)
    ang = jnp.arange(s, dtype=jnp.float32)[:, None] * inv[None, :]
    cos = jnp.cos(ang)[None, :, None, :]
    sin = jnp.sin(ang)[None, :, None, :]
    xf = x.astype(jnp.float32)
    x1, x2 = xf[..., : dr // 2], xf[..., dr // 2:]
    return jnp.concatenate([x1 * cos - x2 * sin, x1 * sin + x2 * cos], axis=-1).astype(x.dtype)

def dilated_branch(q, k, v, window, dilation, slopes):
    b, s, h, dh = q.shape
    n_back = window // dilation
    L = s // dilation
    nb = -(-L // BLOCK)
    Lp = nb * BLOCK

    def to_sub(t):
        t = t.reshape(b, L, dilation, h, dh)
        t = jnp.pad(t, ((0, 0), (0, Lp - L), (0, 0), (0, 0), (0, 0)))
        return t.reshape(b, nb, BLOCK, dilation, h, dh)

    def band(t):
        prev = jnp.pad(t, ((0, 0), (1, 0), (0, 0), (0, 0), (0, 0), (0, 0)))[:, :-1]
        return jnp.concatenate([prev, t], axis=2)

    qs = to_sub(q)
    kb = band(to_sub(k))
    vb = band(to_sub(v)).astype(jnp.float32)
    sc = jnp.einsum('bnqrhd,bnkrhd->bnrhqk', qs, kb, preferred_element_type=jnp.float32) * dh ** -0.5
    qi = jnp.arange(BLOCK)[:, None]
    kk = jnp.arange(2 * BLOCK)[None, :]
    rel = qi + BLOCK - kk
    j_abs = jnp.arange(nb)[:, None, None] * BLOCK - BLOCK + kk[None]
    valid = (rel >= 0)[None] & (rel <= n_back)[None] & (j_abs >= 0)
    bias = -slopes[:, None, None] * (rel * dilation).astype(jnp.float32)[None]
    sc = jnp.where(valid[None, :, None, None], sc + bias[None, None, None], -jnp.inf)
    m = jnp.max(sc, axis=-1)
    p = jnp.exp(sc - m[..., None])
    l = jnp.sum(p, axis=-1)
    o = jnp.einsum('bnrhqk,bnkrhd->bnqrhd', p, vb)
    m = jnp.moveaxis(m, -1, 2)
    l = jnp.moveaxis(l, -1, 2)
    o = o / l[..., None]
    o = o.reshape(b, Lp, dilation, h, dh)[:, :L].reshape(b, s, h, dh)
    m = m.reshape(b, Lp, dilation, h)[:, :L].reshape(b, s, h)
    l = l.reshape(b, Lp, dilation, h)[:, :L].reshape(b, s, h)
    return o, m, l

def dilated_attention(q, k, v):
    slopes = 2.0 ** (-8.0 * jnp.arange(1, A_HEADS + 1, dtype=jnp.float32) / A_HEADS)
    outs = [dilated_branch(q, k, v, w, d, slopes) for (w, d) in A_BRANCHES]
    o_all = jnp.stack([o for o, _, _ in outs])
    m_all = jnp.stack([m for _, m, _ in outs])
    l_all = jnp.stack([l for _, _, l in outs])
    den = l_all * jnp.exp(m_all - jnp.max(m_all, axis=0, keepdims=True))
    alpha = den / jnp.sum(den, axis=0, keepdims=True)
    return jnp.sum(alpha[..., None] * o_all, axis=0)

def to_blocks(t):
    b, s = t.shape[0], t.shape[1]
    return jnp.moveaxis(t.reshape((b, s // BLOCK, BLOCK) + t.shape[2:]), 1, 0)

def from_blocks(t):
    t = jnp.moveaxis(t, 0, 1)
    return t.reshape((t.shape[0], t.shape[1] * t.shape[2]) + t.shape[3:])

def mla_attention(qn, qr, kn, kr, v):
    s = qn.shape[1]
    scale = (B_NOPE_DIM + B_ROPE_DIM) ** -0.5
    kpos = jnp.arange(s)
    vf = v.astype(jnp.float32)

    def one(args):
        qn_b, qr_b, idx = args
        sc = (jnp.einsum('bqhd,bkhd->bhqk', qn_b, kn, preferred_element_type=jnp.float32)
              + jnp.einsum('bqhd,bkd->bhqk', qr_b, kr, preferred_element_type=jnp.float32)) * scale
        qpos = idx * BLOCK + jnp.arange(BLOCK)
        sc = jnp.where(kpos[None, :] <= qpos[:, None], sc, -jnp.inf)
        p = jax.nn.softmax(sc, axis=-1)
        return jnp.einsum('bhqk,bkhd->bqhd', p, vf)

    out = lax.map(one, (to_blocks(qn), to_blocks(qr), jnp.arange(s // BLOCK)))
    return from_blocks(out)

def stick_breaking_attention(q, k, v):
    s, dh = q.shape[1], q.shape[-1]
    kpos = jnp.arange(s)
    vf = v.astype(jnp.float32)

    def one(args):
        q_b, idx = args
        z = jnp.einsum('bqhd,bkhd->bhqk', q_b, k, preferred_element_type=jnp.float32) * dh ** -0.5
        qpos = idx * BLOCK + jnp.arange(BLOCK)
        strict = kpos[None, :] < qpos[:, None]
        log1m = jnp.where(strict, -jax.nn.softplus(z), 0.0)
        later = lax.cumsum(log1m, axis=3, reverse=True) - log1m
        a = jnp.where(strict, jnp.exp(jax.nn.log_sigmoid(z) + later), 0.0)
        return jnp.einsum('bhqk,bkhd->bqhd', a, vf)

    out = lax.map(one, (to_blocks(q), jnp.arange(s // BLOCK)))
    return from_blocks(out)

def mixer_ab(h, w_in, q_norm_g, w_uq, kv_norm_g, w_ukv, w_out):
    b, s, _ = h.shape
    proj = h @ w_in
    a_qkv = proj[..., :A_QKV].reshape(b, s, 3, A_HEADS, A_HEAD_DIM)
    c_q = proj[..., A_QKV:A_QKV + B_Q_RANK]
    c_kv = proj[..., A_QKV + B_Q_RANK:A_QKV + B_Q_RANK + B_KV_RANK]
    k_rope = proj[..., A_QKV + B_Q_RANK + B_KV_RANK:]
    o_a = dilated_attention(a_qkv[:, :, 0], a_qkv[:, :, 1], a_qkv[:, :, 2])
    q = (rmsnorm(c_q, q_norm_g) @ w_uq).reshape(b, s, B_HEADS, B_NOPE_DIM + B_ROPE_DIM)
    kv = (rmsnorm(c_kv, kv_norm_g) @ w_ukv).reshape(b, s, B_HEADS, B_NOPE_DIM + B_V_DIM)
    qn, qr = q[..., :B_NOPE_DIM], rope(q[..., B_NOPE_DIM:])
    kn, vb = kv[..., :B_NOPE_DIM], kv[..., B_NOPE_DIM:]
    kr = rope(k_rope[:, :, None, :])[:, :, 0]
    o_b = mla_attention(qn, qr, kn, kr, vb)
    o = jnp.concatenate([o_a.reshape(b, s, A_HEADS * A_HEAD_DIM),
                         o_b.reshape(b, s, B_HEADS * B_V_DIM)], axis=-1).astype(h.dtype)
    return o @ w_out

def mixer_c(h, w_in, w_out):
    b, s, _ = h.shape
    qkv = (h @ w_in).reshape(b, s, 3, C_HEADS, C_HEAD_DIM)
    o = stick_breaking_attention(qkv[:, :, 0], qkv[:, :, 1], qkv[:, :, 2])
    return o.reshape(b, s, C_OUT).astype(h.dtype) @ w_out

def setup_inputs(seed: int = 0) -> dict:
    key = jax.random.key(seed)
    ks = jax.random.split(key, 16)
    f32 = jnp.float32

    def nrm(k, shape, fan_in):
        return jax.random.normal(k, shape, f32) * fan_in ** -0.5

    def gain(k, shape):
        return 1.0 + 0.02 * jax.random.normal(k, shape, f32)

    return {
        'x': jax.random.normal(ks[0], (BATCH, SEQ, D_MODEL), f32),
        'ffn_norm_g': gain(ks[1], (DEPTH, 2, D_MODEL)),
        'mix_norm_g': gain(ks[2], (DEPTH, D_MODEL)),
        'ffn_w_gate': nrm(ks[3], (DEPTH, 2, D_MODEL, D_FF), D_MODEL),
        'ffn_w_up': nrm(ks[4], (DEPTH, 2, D_MODEL, D_FF), D_MODEL),
        'ffn_w_down': nrm(ks[5], (DEPTH, 2, D_FF, D_MODEL), D_FF),
        'ab_w_in': nrm(ks[6], (N_EVEN, D_MODEL, AB_IN), D_MODEL),
        'mla_q_norm_g': gain(ks[7], (N_EVEN, B_Q_RANK)),
        'mla_w_uq': nrm(ks[8], (N_EVEN, B_Q_RANK, B_HEADS * (B_NOPE_DIM + B_ROPE_DIM)), B_Q_RANK),
        'mla_kv_norm_g': gain(ks[9], (N_EVEN, B_KV_RANK)),
        'mla_w_ukv': nrm(ks[10], (N_EVEN, B_KV_RANK, B_HEADS * (B_NOPE_DIM + B_V_DIM)), B_KV_RANK),
        'ab_w_out': nrm(ks[11], (N_EVEN, AB_OUT, D_MODEL), AB_OUT),
        'sb_w_in': nrm(ks[12], (N_ODD, D_MODEL, C_IN), D_MODEL),
        'sb_w_out': nrm(ks[13], (N_ODD, C_OUT, D_MODEL), C_OUT),
        'final_norm_g': gain(ks[14], (D_MODEL,)),
    }

def reference(x, ffn_norm_g, mix_norm_g, ffn_w_gate, ffn_w_up, ffn_w_down, ab_w_in, mla_q_norm_g,
              mla_w_uq, mla_kv_norm_g, mla_w_ukv, ab_w_out, sb_w_in, sb_w_out, final_norm_g):
    for i in range(DEPTH):
        x = x + 0.5 * swiglu(rmsnorm(x, ffn_norm_g[i, 0]), ffn_w_gate[i, 0], ffn_w_up[i, 0], ffn_w_down[i, 0])
        h = rmsnorm(x, mix_norm_g[i])
        if i % 2 == 0:
            e = i // 2
            x = x + mixer_ab(h, ab_w_in[e], mla_q_norm_g[e], mla_w_uq[e], mla_kv_norm_g[e], mla_w_ukv[e], ab_w_out[e])
        else:
            o = i // 2
            x = x + mixer_c(h, sb_w_in[o], sb_w_out[o])
        x = x + 0.5 * swiglu(rmsnorm(x, ffn_norm_g[i, 1]), ffn_w_gate[i, 1], ffn_w_up[i, 1], ffn_w_down[i, 1])
    return rmsnorm(x, final_norm_g)


_drawn_inputs = setup_inputs


def setup_inputs(seed=0):
    import zlib

    import numpy as np

    out = dict(_drawn_inputs(seed))
    spreads = {}
    factors = {'ffn_norm_g': 3.377,
     'mix_norm_g': 3.655,
     'mla_q_norm_g': 8.0,
     'mla_kv_norm_g': 8.0,
     'final_norm_g': 2.884}
    for name, (base, spread) in spreads.items():
        noise = np.random.default_rng([zlib.crc32(name.encode()), seed]).standard_normal(out[name].shape)
        drawn = base * np.exp(spread * noise) if base else spread * noise
        out[name] = __import__('jax').numpy.asarray(drawn.astype(out[name].dtype))
    for name, factor in factors.items():
        out[name] = (out[name] * factor).astype(out[name].dtype)
    return out
```

```python
import concourse.bass as bass
from concourse import mybir
from contextlib import ExitStack


P = 128
NEG = -1e30


def layout(D, F, SEQ):
    f, b, at_f, at_b = {}, {}, 0, 0
    for name, n in (("ident", P), ("neg_tri", P), ("neg_one", P), ("count", 3 * P),
                    ("cos", 2 * 9 * 16), ("sin", 2 * 9 * 16)):
        f[name] = (at_f, at_f + n)
        at_f += n
    for name, n in (("identb", P), ("slopes", 8 * P), ("dist", 3 * P), ("causal", 3 * P), ("strict", 3 * P)):
        b[name] = (at_b, at_b + n)
        at_b += n
    return f, at_f, b, at_b


def trunk_kernel(nc, x, ffn_norm_g, mix_norm_g, w_gate, w_up, w_down, ab_w_in, q_norm_g, w_uq, kv_norm_g,
                 w_ukv, ab_w_out, sb_w_in, sb_w_out, final_norm_g, table_f, table_b, out):
    fp32, f32r, bf16, u16 = mybir.dt.float32, mybir.dt.float32r, mybir.dt.bfloat16, mybir.dt.uint16
    ALU, ACT, AX = mybir.AluOpType, mybir.ActivationFunctionType, mybir.AxisListType

    _, SEQ, D = x.shape
    F = w_gate.shape[-1]
    EPS = 1e-6
    NT = SEQ // P
    KT = D // P
    HALF = D // 2
    CH = 256
    NCH = F // CH
    FT = CH // P
    KS = ((0, 3), (3, 6), (6, 8))
    DH = 64
    H_A, H_B, H_C = 8, 8, 16
    QD, ROPE = 96, 32
    RQ, RKV = q_norm_g.shape[-1], kv_norm_g.shape[-1]
    LAT = RQ + RKV + ROPE
    A_QKV = 3 * H_A * DH
    PAIRS_A, PAIRS_C = H_A // 2, H_C // 2
    G_Q = 6 * KT
    G_KV = G_Q + RQ // P
    N_G = G_KV + RKV // P

    ctx = ExitStack()
    with ctx:
        def sb(name, shape, dt=fp32):
            return ctx.enter_context(nc.sbuf_tensor(name, shape, dt))

        def sem(name):
            return ctx.enter_context(nc.semaphore(name))

        raw = [sb(f"raw{s}", [P, 2048]) for s in range(3)]
        w_hi = [sb(f"w_hi{s}", [P, 2048], f32r) for s in range(3)]
        w_lo = [sb(f"w_lo{s}", [P, 2048], f32r) for s in range(3)]
        xres = sb("xres", [P, NT, D])
        rows = sb("rows", [P, NT, D])
        t_hi = sb("t_hi", [P, KT, SEQ], f32r)
        t_lo = sb("t_lo", [P, KT, SEQ], f32r)
        junk = sb("junk", [P, D])
        hid = sb("hid", [P, NT, CH])
        gate = sb("gate", [P, NT, CH])
        h_hi = sb("h_hi", [P, FT, SEQ], f32r)
        h_lo = sb("h_lo", [P, FT, SEQ], f32r)
        ss = sb("ss", [P, NT])
        ms = sb("ms", [P, NT])
        rstd = sb("rstd", [P, NT])
        half_neg = sb("half_neg", [P, 4])
        g_rows = sb("g_rows", [P, P])
        g_col = sb("g_col", [P, P])
        g_fin = sb("g_fin", [P, D])
        FC, nf, BC, nb = layout(D, F, SEQ)
        tabf = sb("tabf", [P, nf])
        tabb = sb("tabb", [P, nb], bf16)
        qk_t = sb("qk_t", [P, 2 * SEQ])
        pr = [sb(f"pr{e}", [P, 3 * P]) for e in range(2)]
        pc = [sb(f"pc{e}", [P, 3 * P]) for e in range(2)]
        pt = [sb(f"pt{e}", [P, 3 * P]) for e in range(2)]
        nmax = sb("nmax", [P, 2, NT])
        rden = sb("rden", [P, NT, 2, 1])
        v_a = sb("v_a", [P, NT, H_A * (DH + 1)])
        v_b = sb("v_b", [P, NT, H_B * (DH + 1)])
        v_c = sb("v_c", [P, NT, H_C * DH])
        lat = sb("lat", [P, NT, RQ + RKV])
        lat_ss = sb("lat_ss", [P, NT, 2])
        lat_ms = sb("lat_ms", [P, NT, 2])
        lat_rstd = sb("lat_rstd", [P, NT, 2])
        lt_hi = sb("lt_hi", [P, 3, SEQ], f32r)
        lt_lo = sb("lt_lo", [P, 3, SEQ], f32r)
        q_b = sb("q_b", [P, NT, 9 * QD])
        k_b = sb("k_b", [P, NT, H_B * QD])
        rot = [sb(f"rot{i}", [P, NT, 9, 16]) for i in range(4)]
        q_st = sb("q_st", [P, NT, 2 * QD])
        k_st = sb("k_st", [P, NT, 2 * QD])
        qk_b = [sb(f"qk_b{e}", [P, 2 * SEQ]) for e in range(2)]
        sp_abs = [sb(f"sp_abs{e}", [P, 3 * P]) for e in range(2)]
        sp_exp = [sb(f"sp_exp{e}", [P, 3 * P]) for e in range(2)]
        sp = [sb(f"sp{e}", [P, 3 * P]) for e in range(2)]

        bank = [ctx.enter_context(nc.psum_tensor(f"bank{i}", [P, 512], fp32)) for i in range(8)]
        acc = [[bank[4 + 2 * t + h] for h in range(2)] for t in range(NT)]

        def tf(name):
            return tabf[:, FC[name][0]:FC[name][1]]

        def tb(name, lo=0, hi=None):
            a, b = BC[name]
            return tabb[:, a + lo:(b if hi is None else a + hi)]

        ident = tf("ident")

        s_in = sem("x_loaded")
        s_tab = sem("tables_loaded")
        s_gr = sem("gain_rows_loaded")
        s_gf = sem("final_gain_loaded")
        s_raw = [sem(f"raw_loaded{s}") for s in range(3)]
        s_hi = [sem(f"high_ready{s}") for s in range(3)]
        s_lo = [sem(f"low_ready{s}") for s in range(3)]
        s_used = [sem(f"weights_used{s}") for s in range(3)]
        s_half = sem("constants_set")
        s_gt = sem("gains_transposed")
        s_gc = sem("gains_ready")
        s_acc = sem("sublayer_summed")
        s_x = sem("residual_updated")
        s_ss = sem("squares_summed")
        s_ms = sem("mean_square_ready")
        s_rs = sem("rstd_ready")
        s_xn = sem("rows_normed")
        s_xt = sem("rows_transposed")
        s_th = sem("transpose_high_ready")
        s_tl = sem("transpose_low_ready")
        s_gu = sem("gate_up_summed")
        s_sg = sem("silu_ready")
        s_h = sem("hidden_ready")
        s_ht = sem("hidden_transposed")
        s_hh = sem("hidden_high_ready")
        s_hl = sem("hidden_low_ready")
        s_vc = sem("v_copied")
        s_qkc = sem("qk_copied")
        s_lss = sem("latent_squares_summed")
        s_lms = sem("latent_mean_square_ready")
        s_lrs = sem("latent_rstd_ready")
        s_ln = sem("latents_normed")
        s_lt = sem("latents_transposed")
        s_lth = sem("latent_high_ready")
        s_ltl = sem("latent_low_ready")
        s_qb = sem("mla_q_copied")
        s_kb = sem("mla_k_copied")
        s_vb = sem("mla_v_copied")
        s_rt = sem("rotary_products_ready")
        s_ro = sem("rotary_applied")
        s_kr = sem("mla_k_complete")
        s_st = sem("mla_pair_staged")
        s_tq = sem("mla_pair_transposed")
        s_qbt = [sem(f"mla_head_ready{e}") for e in range(2)]
        s_sc = sem("scores_ready")
        s_mx = sem("max_ready")
        s_ex = sem("exp_ready")
        s_cn = sem("counted")
        s_pt = sem("probs_transposed")
        s_pe = [sem(f"probs_copied{e}") for e in range(2)]
        s_pv = sem("pv_summed")
        s_rd = sem("denominators_inverted")
        s_on = sem("outputs_normed")
        s_z = sem("z_ready")
        s_za = sem("z_abs_ready")
        s_ze = sem("z_exp_ready")
        s_zl = sem("z_log_ready")
        s_sp = sem("softplus_ready")
        s_cs = sem("logits_ready")
        s_at = sem("weights_ready")
        s_oc = sem("stick_summed")
        s_oe = sem("stick_copied")
        s_y = sem("final_rows_ready")
        s_out = sem("stored")

        block = ctx.enter_context(nc.Block())

        FFN_ROUNDS, A_ROUNDS, C_ROUNDS = NCH, 3 + PAIRS_A + 2, 2 + PAIRS_C + 2
        R_FFN = [0, FFN_ROUNDS + A_ROUNDS, 2 * FFN_ROUNDS + A_ROUNDS, 3 * FFN_ROUNDS + A_ROUNDS + C_ROUNDS]
        R_AB = FFN_ROUNDS
        R_C = 3 * FFN_ROUNDS + A_ROUNDS
        NORM_FFN, NORM_AB, NORM_C, NORM_END = [0, 2, 3, 5], 1, 4, 6
        R_NORM = [0, R_AB, R_FFN[1], R_FFN[2], R_C, R_FFN[3], R_FFN[3] + NCH]
        T_FFN, T_AB, T_AB_O, T_C, T_C_O = [0, 3, 4, 7], 1, 2, 5, 6

        @block.sync
        def _(sp_):
            def load(slot, r, parts):
                if not (isinstance(r, int) and r == 0):
                    sp_.wait_ge(s_lo[slot], r)
                for dst, src in parts:
                    sp_.dma_start(dst, src).then_inc(s_raw[slot], 16)

            def load_up(f, r0, c, slot):
                kt = slice(4 * slot, 4 * slot + 4)
                dst = raw[slot][:, :].rearrange("p (k b n) -> p k b n", k=4, b=2)
                load(slot, r0 + c, [
                    (dst[:, :, b, :], w[f // 2, f % 2].rearrange("(k p) n -> p k n", p=P)[:, kt, bass.ds(c * CH, CH)])
                    for b, w in ((0, w_gate), (1, w_up))])

            def load_down(f, r0, c):
                src = w_down[f // 2, f % 2]
                load(2, r0 + c, [
                    (raw[2][:, i * D:(i + 1) * D], src[bass.ds(c * CH + i * P, P), :]) for i in range(FT)])

            def load_ffn(f):
                r0 = R_FFN[f]
                for s in range(2):
                    load_up(f, r0, 0, s)
                with sp_.Fori(1, NCH) as c:
                    for s in range(2):
                        load_up(f, r0, c, s)
                    load_down(f, r0, c - 1)
                load_down(f, r0, NCH - 1)

            def load_block(w, r, col, n):
                src = w.rearrange("(k p) n -> p k n", p=P)
                for s, (a, b) in enumerate(KS):
                    dst = raw[s][:, 0:(b - a) * n].rearrange("p (k n) -> p k n", k=b - a)
                    load(s, r, [(dst[:, 0:1, :], src[:, a:a + 1, bass.ds(col, n)]),
                                (dst[:, 1:, :], src[:, a + 1:b, bass.ds(col, n)])])

            def load_qk(w, r, j, width):
                src = w.rearrange("(k p) n -> p k n", p=P)
                for s, (a, b) in enumerate(KS):
                    dst = raw[s][:, 0:(b - a) * 2 * P].rearrange("p (k b n) -> p k b n", k=b - a, b=2)
                    load(s, r, [(dst[:, :, i, :], src[:, a:b, bass.ds(j * P + i * width, P)]) for i in range(2)])

            for t in range(NT):
                sp_.dma_start(xres[:, t, :], x[0, t * P:(t + 1) * P, :]).then_inc(s_in, 16)
            load_up(0, 0, 0, 0)
            sp_.dma_start(tabf[:, :], table_f).then_inc(s_tab, 16)
            for l in range(2):
                for s in range(2):
                    k = (2 * l + s) * KT
                    sp_.dma_start(g_rows[k:k + KT, :], ffn_norm_g[l, s].rearrange("(k p) -> k p", p=P)).then_inc(s_gr, 16)
                k = (4 + l) * KT
                sp_.dma_start(g_rows[k:k + KT, :], mix_norm_g[l].rearrange("(k p) -> k p", p=P)).then_inc(s_gr, 16)
            sp_.dma_start(g_rows[G_Q:G_KV, :], q_norm_g[0].rearrange("(k p) -> k p", p=P)).then_inc(s_gr, 16)
            sp_.dma_start(g_rows[G_KV:N_G, :], kv_norm_g[0].rearrange("(k p) -> k p", p=P)).then_inc(s_gr, 16)
            load_up(0, 0, 0, 1)
            sp_.dma_start(tabb[:, :].bitcast(u16), table_b).then_inc(s_tab, 16)
            sp_.dma_start(g_fin[:, :], final_norm_g.partition_broadcast(P)).then_inc(s_gf, 16)

            with sp_.Fori(1, NCH) as c:
                for s in range(2):
                    load_up(0, 0, c, s)
                load_down(0, 0, c - 1)
            load_down(0, 0, NCH - 1)
            load_block(ab_w_in[0], R_AB, A_QKV, LAT)
            load_block(ab_w_in[0], R_AB + 1, 2 * H_A * DH, H_A * DH)
            for s in range(RQ // P):
                n = H_B * QD // 2
                load(s, R_AB + 2, [(raw[s][:, i * n:(i + 1) * n], w_uq[0, s * P:(s + 1) * P, i * n:(i + 1) * n])
                                   for i in range(2)])
            n = H_B * 2 * DH // 2
            load(2, R_AB + 2, [(raw[2][:, i * n:(i + 1) * n], w_ukv[0, :, i * n:(i + 1) * n]) for i in range(2)])
            with sp_.Fori(0, PAIRS_A) as j:
                load_qk(ab_w_in[0], R_AB + 3 + j, j, H_A * DH)
            with sp_.Fori(0, 2) as j:
                load_block(ab_w_out[0], R_AB + 3 + PAIRS_A + j, j * HALF, HALF)
            load_ffn(1)
            load_ffn(2)
            with sp_.Fori(0, 2) as j:
                load_block(sb_w_in[0], R_C + j, 2 * D + j * HALF, HALF)
            with sp_.Fori(0, PAIRS_C) as j:
                load_qk(sb_w_in[0], R_C + 2 + j, j, D)
            with sp_.Fori(0, 2) as j:
                load_block(sb_w_out[0], R_C + 2 + PAIRS_C + j, j * HALF, HALF)
            load_ffn(3)
            for t in range(NT):
                sp_.wait_ge(s_y, t + 1)
                sp_.dma_start(out[0, t * P:(t + 1) * P, :], rows[:, t, :]).then_inc(s_out, 16)
            sp_.wait_ge(s_out, 16 * NT)

        @block.gpsimd
        def _(pool):
            nc.gpsimd.memset(half_neg[:, :], -0.5).then_inc(s_half, 1)
            nc.gpsimd.memset(v_a[:, :, :], 1.0).then_inc(s_half, 1)
            nc.gpsimd.memset(v_b[:, :, :], 1.0).then_inc(s_half, 1)
            pool.wait_ge(s_half, 3)

            def root(n):
                for t in range(NT):
                    pool.wait_ge(s_ms, NT * n + t + 1)
                    nc.gpsimd.tensor_tensor(rstd[:, t:t + 1], ms[:, t:t + 1], half_neg[:, 0:1], ALU.pow).then_inc(s_rs, 1)

            root(NORM_FFN[0])
            root(NORM_AB)
            pool.wait_ge(s_lms, 2)
            nc.gpsimd.tensor_tensor(lat_rstd[:, :, :].rearrange("p t n -> p (t n)"),
                                    lat_ms[:, :, :].rearrange("p t n -> p (t n)"), half_neg[:, :], ALU.pow).then_inc(s_lrs, 1)
            pool.wait_ge(s_tab, 32)
            pool.wait_ge(s_ro, 2)
            pool.wait_ge(s_kr, 1)
            with pool.Fori(0, PAIRS_A) as j:
                pool.wait_ge(s_tq, j + 1)
                nc.gpsimd.tensor_copy(q_st[:, :, :], q_b[:, :, bass.ds(j * (2 * QD), 2 * QD)]).then_inc(s_st, 1)
                nc.gpsimd.tensor_copy(k_st[:, :, :], k_b[:, :, bass.ds(j * (2 * QD), 2 * QD)]).then_inc(s_st, 1)
                for e in range(2):
                    pool.wait_ge(s_ex, j * 4 + (e + 1))
                    nc.gpsimd.tensor_tensor(pc[e][:, :], pr[e][:, :], tf("count"), ALU.mult).then_inc(s_cn, 1)
            for n in (2, 3, 4, 5, 6):
                root(n)

        @block.scalar
        def _(act):
            A = nc.scalar.activation

            def split_hi(slot, r, n):
                act.wait_ge(s_raw[slot], r * 32 + 32)
                if not (isinstance(r, int) and r == 0):
                    act.wait_ge(s_used[slot], r)
                A(w_hi[slot][:, 0:n], raw[slot][:, 0:n], ACT.Copy).then_inc(s_hi[slot], 1)

            def squares(n):
                for t in range(NT):
                    if n == 0:
                        act.wait_ge(s_in, 16 * NT)
                    else:
                        act.wait_ge(s_x, NT * (n - 1) + t + 1)
                    if NT * n + t:
                        act.wait_ge(s_ss, NT * n + t)
                    A(junk[:, :], xres[:, t, :], ACT.Square, accum_out=ss[:, t:t + 1]).then_inc(s_ss, 1)

            def transposed_hi(k, g0):
                act.wait_ge(s_xt, NT * (k + 1))
                if k == 0:
                    act.wait_ge(s_gc, 1)
                for i in range(KT):
                    src = bank[i // 2][:, (i % 2) * SEQ:(i % 2 + 1) * SEQ]
                    if g0 is None:
                        A(t_hi[:, i, :], src, ACT.Copy).then_inc(s_th, 1)
                    else:
                        A(t_hi[:, i, :], src, ACT.Copy, scale=g_col[:, g0 + i:g0 + i + 1]).then_inc(s_th, 1)

            def ffn(f):
                r0, b = R_FFN[f], f * NCH
                split_hi(0, r0, 2048)
                split_hi(1, r0, 2048)
                squares(NORM_FFN[f])
                transposed_hi(T_FFN[f], f * KT)

                def silu(c):
                    for t in range(NT):
                        if t == 0:
                            act.wait_ge(s_gu, c + (b + 1))
                        else:
                            act.wait_ge(s_used[1], c + (r0 + 1))
                        A(gate[:, t, :], bank[t][:, 0:CH], ACT.Silu).then_inc(s_sg, 1)

                def hidden_hi(c):
                    act.wait_ge(s_ht, c + (b + 1))
                    A(h_hi[:, :, :].rearrange("p k n -> p (k n)"), bank[2][:, :], ACT.Copy).then_inc(s_hh, 1)

                with act.Fori(1, NCH) as c:
                    split_hi(0, c + r0, 2048)
                    silu(c - 1)
                    split_hi(1, c + r0, 2048)
                    hidden_hi(c - 1)
                    split_hi(2, c + (r0 - 1), 2048)
                silu(NCH - 1)
                hidden_hi(NCH - 1)
                split_hi(2, r0 + NCH - 1, 2048)

            act.wait_ge(s_gt, 1)
            A(g_col[:, 0:N_G], bank[7][:, 0:N_G], ACT.Copy).then_inc(s_gc, 1)
            ffn(0)

            r = R_AB
            for s, (a, b) in enumerate(KS):
                split_hi(s, r, (b - a) * LAT)
            squares(NORM_AB)
            transposed_hi(T_AB, 4 * KT)
            for s, (a, b) in enumerate(KS):
                split_hi(s, r + 1, (b - a) * H_A * DH)
            act.wait_ge(s_used[2], r + 1)
            for t in range(NT):
                for i, (a, n) in enumerate(((0, RQ), (RQ, RKV))):
                    act.wait_ge(s_ss, 2 * NT) if t + i == 0 else act.wait_ge(s_lss, 2 * t + i)
                    A(junk[:, 0:n], bank[t][:, a:a + n], ACT.Square, accum_out=lat_ss[:, t, i:i + 1]).then_inc(s_lss, 1)
            for t in range(NT):
                A(q_b[:, t, 8 * QD + DH:9 * QD], bank[t][:, RQ + RKV:LAT], ACT.Copy).then_inc(s_qb, 1)
            act.wait_ge(s_lt, 1)
            for i in range(3):
                A(lt_hi[:, i, :], bank[2 + i // 2][:, (i % 2) * SEQ:(i % 2 + 1) * SEQ], ACT.Copy,
                  scale=g_col[:, G_Q + i:G_Q + i + 1]).then_inc(s_lth, 1)
            split_hi(0, r + 2, H_B * QD)
            split_hi(1, r + 2, H_B * QD)
            split_hi(2, r + 2, H_B * 2 * DH)
            act.wait_ge(s_used[2], r + 2)
            act.wait_ge(s_half, 3)
            for t in range(NT):
                A(v_a[:, t, :].rearrange("p (h d) -> p h d", d=DH + 1)[:, :, 0:DH],
                  bank[4 + t][:, :].rearrange("p (h d) -> p h d", d=DH), ACT.Copy).then_inc(s_vc, 1)
            act.wait_ge(s_used[1], r + 3)
            for t in range(NT):
                for i in range(2):
                    A(q_b[:, t, i * 4 * QD:(i + 1) * 4 * QD], bank[(6, 4)[t] + i][:, 0:4 * QD], ACT.Copy,
                      scale=float(QD) ** -0.5).then_inc(s_qb, 1)
            act.wait_ge(s_used[2], r + 3)
            for t in range(NT):
                for i in range(2):
                    A(v_b[:, t, i * 4 * (DH + 1):(i + 1) * 4 * (DH + 1)].rearrange("p (h d) -> p h d", d=DH + 1)[:, :, 0:DH],
                      bank[2 * t + i][:, :].rearrange("p (h d) -> p h d", d=2 * DH)[:, :, DH:2 * DH],
                      ACT.Copy).then_inc(s_vb, 1)
            for s, (a, b) in enumerate(KS):
                split_hi(s, r + 3, (b - a) * 2 * P)
            act.wait_ge(s_used[2], r + 4)
            A(qk_t[:, 0:SEQ], bank[4][:, 0:SEQ], ACT.Copy, scale=DH ** -0.5).then_inc(s_qkc, 1)
            A(qk_t[:, SEQ:], bank[4][:, SEQ:], ACT.Copy).then_inc(s_qkc, 1)

            def exps(n, e):
                act.wait_ge(s_mx, 2 * n + (e + 1))
                A(pr[e][:, 0:P], bank[e][:, 0:P], ACT.Exp, bias=nmax[:, e, 0:1])
                A(pr[e][:, P:], bank[e][:, P:3 * P], ACT.Exp, bias=nmax[:, e, 1:2]).then_inc(s_ex, 1)

            def ab_pair(j, more):
                if more:
                    split_hi(0, j + (r + 4), 3 * 2 * P)
                for e in range(2):
                    exps(2 * j, e)
                act.wait_ge(s_tq, 2 + j)
                A(qk_b[0][0:QD, :], bank[5][0:QD, :], ACT.Copy).then_inc(s_qbt[0], 1)
                if more:
                    split_hi(1, j + (r + 4), 3 * 2 * P)
                act.wait_ge(s_pt, 4 * j + 1)
                A(pt[0][:, :], bank[2][:, 0:3 * P], ACT.Copy).then_inc(s_pe[0], 1)
                for e in range(2):
                    exps(2 * j + 1, e)
                if more:
                    split_hi(2, j + (r + 4), 2 * 2 * P)
                act.wait_ge(s_pt, 4 * j + 3)
                act.wait_ge(s_pv, 2 * j + 1)
                A(pt[0][:, :], bank[2][:, 0:3 * P], ACT.Copy).then_inc(s_pe[0], 1)
                if more:
                    act.wait_ge(s_used[2], j + (r + 5))
                    A(qk_t[:, 0:SEQ], bank[4][:, 0:SEQ], ACT.Copy, scale=DH ** -0.5).then_inc(s_qkc, 1)
                    A(qk_t[:, SEQ:], bank[4][:, SEQ:], ACT.Copy).then_inc(s_qkc, 1)

            with act.Fori(0, PAIRS_A - 1) as j:
                ab_pair(j, True)
            ab_pair(PAIRS_A - 1, False)
            r = R_AB + 3 + PAIRS_A
            for s, (a, b) in enumerate(KS):
                split_hi(s, r, (b - a) * HALF)
            transposed_hi(T_AB_O, None)
            for s, (a, b) in enumerate(KS):
                split_hi(s, r + 1, (b - a) * HALF)

            ffn(1)
            ffn(2)

            r = R_C
            for s, (a, b) in enumerate(KS):
                split_hi(s, r, (b - a) * HALF)
            squares(NORM_C)
            transposed_hi(T_C, 5 * KT)
            for s, (a, b) in enumerate(KS):
                split_hi(s, r + 1, (b - a) * HALF)
            for n in range(2):
                act.wait_ge(s_used[2], r + n + 1)
                for t in range(NT):
                    A(v_c[:, t, n * HALF:(n + 1) * HALF], bank[2 * n + t][:, :], ACT.Copy).then_inc(s_vc, 1)
                if n == 0:
                    for s, (a, b) in enumerate(KS):
                        split_hi(s, r + 2, (b - a) * 2 * P)

            def c_qk(j):
                act.wait_ge(s_used[2], j + (r + 3))
                A(qk_t[:, 0:SEQ], bank[4][:, 0:SEQ], ACT.Copy, scale=DH ** -0.5).then_inc(s_qkc, 1)
                A(qk_t[:, SEQ:], bank[4][:, SEQ:], ACT.Copy).then_inc(s_qkc, 1)

            c_qk(0)

            def c_pair(j, more):
                n = 2 * j
                if more:
                    split_hi(0, j + (r + 3), 3 * 2 * P)
                for e in range(2):
                    act.wait_ge(s_z, n + (e + 1))
                    A(sp_abs[e][:, :], bank[e][:, 0:3 * P], ACT.Abs).then_inc(s_za, 1)
                if more:
                    split_hi(1, j + (r + 3), 3 * 2 * P)
                for e in range(2):
                    act.wait_ge(s_za, n + (e + 1))
                    A(sp_exp[e][:, :], sp_abs[e][:, :], ACT.Exp, scale=-1.0).then_inc(s_ze, 1)
                for e in range(2):
                    act.wait_ge(s_ze, n + (e + 1))
                    A(sp_abs[e][:, :], sp_exp[e][:, :], ACT.Ln, bias=1.0).then_inc(s_zl, 1)
                if more:
                    split_hi(2, j + (r + 3), 2 * 2 * P)
                for e in range(2):
                    act.wait_ge(s_cs, n + (e + 1))
                    A(pr[e][:, :], bank[e][:, 0:3 * P], ACT.Exp).then_inc(s_at, 1)
                if more:
                    c_qk(j + 1)
                act.wait_ge(s_oc, j + 1)
                A(rows[:, :, bass.ds(j * P, P)], bank[3][:, 0:SEQ].rearrange("p (t n) -> p t n", t=NT),
                  ACT.Copy).then_inc(s_oe, 1)

            with act.Fori(0, PAIRS_C - 1) as j:
                c_pair(j, True)
            c_pair(PAIRS_C - 1, False)
            r = R_C + 2 + PAIRS_C
            for s, (a, b) in enumerate(KS):
                split_hi(s, r, (b - a) * HALF)
            transposed_hi(T_C_O, None)
            for s, (a, b) in enumerate(KS):
                split_hi(s, r + 1, (b - a) * HALF)
            ffn(3)
            squares(NORM_END)

        @block.vector
        def _(dve):
            V = nc.vector

            def split_lo(slot, r, n):
                dve.wait_ge(s_hi[slot], r + 1)
                V.tensor_tensor(w_lo[slot][:, 0:n], raw[slot][:, 0:n], w_hi[slot][:, 0:n].bitcast(fp32),
                                ALU.subtract).then_inc(s_lo[slot], 1)

            def residual(n, scale):
                for t in range(NT):
                    if t == 0:
                        dve.wait_ge(s_acc, n)
                    else:
                        dve.wait_ge(s_used[2], R_NORM[n])
                    for h in range(2):
                        xs = xres[:, t, h * HALF:(h + 1) * HALF]
                        last = V.scalar_tensor_tensor(out=xs, in0=acc[t][h][:, :], scalar=scale, in1=xs,
                                                      op0=ALU.mult, op1=ALU.add)
                    last.then_inc(s_x, 1)

            def means(n):
                for t in range(NT):
                    dve.wait_ge(s_ss, NT * n + t + 1)
                    V.tensor_scalar(ms[:, t:t + 1], ss[:, t:t + 1], 1.0 / D, EPS, op0=ALU.mult, op1=ALU.add).then_inc(s_ms, 1)

            def norm(n):
                means(n)
                for t in range(NT):
                    dve.wait_ge(s_rs, NT * n + t + 1)
                    V.tensor_scalar(rows[:, t, :], xres[:, t, :], rstd[:, t:t + 1], None, op0=ALU.mult).then_inc(s_xn, 1)

            def transposed_lo(k, g0):
                for i in range(KT):
                    if i % 2 == 0:
                        dve.wait_ge(s_th, KT * k + i + 2)
                    src = bank[i // 2][:, (i % 2) * SEQ:(i % 2 + 1) * SEQ]
                    hi = t_hi[:, i, :].bitcast(fp32)
                    if g0 is None:
                        V.tensor_tensor(t_lo[:, i, :], src, hi, ALU.subtract).then_inc(s_tl, 1)
                    else:
                        V.scalar_tensor_tensor(out=t_lo[:, i, :], in0=src, scalar=g_col[:, g0 + i:g0 + i + 1], in1=hi,
                                               op0=ALU.mult, op1=ALU.subtract).then_inc(s_tl, 1)

            def ffn(f, scale):
                r0, b = R_FFN[f], f * NCH
                split_lo(0, r0, 2048)
                split_lo(1, r0, 2048)
                if f:
                    residual(NORM_FFN[f], scale)
                norm(NORM_FFN[f])
                transposed_lo(T_FFN[f], f * KT)

                def hidden(c):
                    for t in range(NT):
                        dve.wait_ge(s_sg, (c + b) * NT + (t + 1))
                        V.tensor_tensor(hid[:, t, :], bank[t][:, CH:2 * CH], gate[:, t, :], ALU.mult).then_inc(s_h, 1)

                def hidden_lo(c):
                    dve.wait_ge(s_hh, c + (b + 1))
                    V.tensor_tensor(h_lo[:, :, :].rearrange("p k n -> p (k n)"), bank[2][:, :],
                                    h_hi[:, :, :].rearrange("p k n -> p (k n)").bitcast(fp32), ALU.subtract).then_inc(s_hl, 1)

                with dve.Fori(1, NCH) as c:
                    split_lo(0, c + r0, 2048)
                    hidden(c - 1)
                    split_lo(1, c + r0, 2048)
                    hidden_lo(c - 1)
                    split_lo(2, c + (r0 - 1), 2048)
                hidden(NCH - 1)
                hidden_lo(NCH - 1)
                split_lo(2, r0 + NCH - 1, 2048)

            ffn(0, None)

            r = R_AB
            for s, (a, b) in enumerate(KS):
                split_lo(s, r, (b - a) * LAT)
            residual(NORM_AB, 0.5)
            norm(NORM_AB)
            transposed_lo(T_AB, 4 * KT)
            for s, (a, b) in enumerate(KS):
                split_lo(s, r + 1, (b - a) * H_A * DH)
            dve.wait_ge(s_lss, 4)
            for i, n in enumerate((RQ, RKV)):
                V.tensor_scalar(lat_ms[:, :, i:i + 1], lat_ss[:, :, i:i + 1], 1.0 / n, EPS, op0=ALU.mult, op1=ALU.add).then_inc(s_lms, 1)
            dve.wait_ge(s_lrs, 1)
            dve.wait_ge(s_qb, 2)
            for t in range(NT):
                for i, (a, n) in enumerate(((0, RQ), (RQ, RKV))):
                    V.tensor_scalar(lat[:, t, a:a + n], bank[t][:, a:a + n], lat_rstd[:, t, i:i + 1], None, op0=ALU.mult).then_inc(s_ln, 1)
            for i in range(3):
                dve.wait_ge(s_lth, (2, 2, 3)[i])
                V.scalar_tensor_tensor(out=lt_lo[:, i, :], in0=bank[2 + i // 2][:, (i % 2) * SEQ:(i % 2 + 1) * SEQ],
                                       scalar=g_col[:, G_Q + i:G_Q + i + 1], in1=lt_hi[:, i, :].bitcast(fp32),
                                       op0=ALU.mult, op1=ALU.subtract).then_inc(s_ltl, 1)
            split_lo(0, r + 2, H_B * QD)
            split_lo(1, r + 2, H_B * QD)
            split_lo(2, r + 2, H_B * 2 * DH)
            dve.wait_ge(s_used[2], r + 3)
            for t in range(NT):
                for i in range(2):
                    dve.wait_ge(s_vb, 2 * t + i + 1)
                    V.tensor_copy(k_b[:, t, i * 4 * QD:(i + 1) * 4 * QD].rearrange("p (h d) -> p h d", d=QD)[:, :, 0:DH],
                                  bank[2 * t + i][:, :].rearrange("p (h d) -> p h d", d=2 * DH)[:, :, 0:DH]).then_inc(s_kb, 1)
            for s, (a, b) in enumerate(KS):
                split_lo(s, r + 3, (b - a) * 2 * P)
            dve.wait_ge(s_qb, 2 + 4)
            dve.wait_ge(s_tab, 32)
            q9 = q_b[:, :, :].rearrange("p t (h d) -> p t h d", d=QD)
            x1, x2 = q9[:, :, :, DH:DH + 16], q9[:, :, :, DH + 16:QD]
            cos, sin = (tf(n).rearrange("p (t h d) -> p t h d", t=NT, h=9) for n in ("cos", "sin"))
            for i, (u, w) in enumerate(((x1, cos), (x2, sin), (x1, sin), (x2, cos))):
                V.tensor_tensor(rot[i][:, :, :, :], u, w, ALU.mult).then_inc(s_rt, 1)
            dve.wait_ge(s_rt, 4)
            V.tensor_tensor(x1, rot[0][:, :, :, :], rot[1][:, :, :, :], ALU.subtract).then_inc(s_ro, 1)
            V.tensor_tensor(x2, rot[2][:, :, :, :], rot[3][:, :, :, :], ALU.add).then_inc(s_ro, 1)
            dve.wait_ge(s_ro, 2)
            kr = q9[:, :, 8:9, DH:QD].to_broadcast([P, NT, H_B, ROPE])
            V.tensor_copy(k_b[:, :, :].rearrange("p t (h d) -> p t h d", d=QD)[:, :, :, DH:QD], kr).then_inc(s_kr, 1)

            def maxima(n, e):
                dve.wait_ge(s_sc, 2 * n + (e + 1))
                V.tensor_reduce(nmax[:, e, 0:1], bank[e][:, 0:P], AX.X, ALU.max, negate=True)
                V.tensor_reduce(nmax[:, e, 1:2], bank[e][:, P:3 * P], AX.X, ALU.max, negate=True).then_inc(s_mx, 1)

            def outputs(n, col):
                dve.wait_ge(s_pv, n + 1)
                o = bank[7][:, 0:4 * (DH + 1)].rearrange("p (t h d) -> p t h d", t=NT, h=2)
                V.reciprocal(rden[:, :, :, :], o[:, :, :, DH:DH + 1]).then_inc(s_rd, 1)
                dve.wait_ge(s_rd, n + 1)
                V.tensor_tensor(rows[:, :, bass.ds(col, P)].rearrange("p t (h d) -> p t h d", h=2), o[:, :, :, 0:DH],
                                rden[:, :, :, :].to_broadcast([P, NT, 2, DH]), ALU.mult).then_inc(s_on, 1)

            def ab_pair(j, more):
                if more:
                    split_lo(0, j + (r + 4), 3 * 2 * P)
                for e in range(2):
                    maxima(2 * j, e)
                dve.wait_ge(s_tq, 2 + j)
                V.tensor_copy(qk_b[1][0:QD, :], bank[6][0:QD, :]).then_inc(s_qbt[1], 1)
                if more:
                    split_lo(1, j + (r + 4), 3 * 2 * P)
                dve.wait_ge(s_pt, 4 * j + 2)
                V.tensor_copy(pt[1][:, :], bank[3][:, 0:3 * P]).then_inc(s_pe[1], 1)
                for e in range(2):
                    maxima(2 * j + 1, e)
                if more:
                    split_lo(2, j + (r + 4), 2 * 2 * P)
                outputs(2 * j, j * P)
                dve.wait_ge(s_pt, 4 * j + 4)
                V.tensor_copy(pt[1][:, :], bank[3][:, 0:3 * P]).then_inc(s_pe[1], 1)
                outputs(2 * j + 1, j * P + HALF)

            with dve.Fori(0, PAIRS_A - 1) as j:
                ab_pair(j, True)
            ab_pair(PAIRS_A - 1, False)
            r = R_AB + 3 + PAIRS_A
            for s, (a, b) in enumerate(KS):
                split_lo(s, r, (b - a) * HALF)
            transposed_lo(T_AB_O, None)
            for s, (a, b) in enumerate(KS):
                split_lo(s, r + 1, (b - a) * HALF)

            ffn(1, 1.0)
            ffn(2, 0.5)

            r = R_C
            for s, (a, b) in enumerate(KS):
                split_lo(s, r, (b - a) * HALF)
            residual(NORM_C, 0.5)
            norm(NORM_C)
            transposed_lo(T_C, 5 * KT)
            for s, (a, b) in enumerate(KS):
                split_lo(s, r + 1, (b - a) * HALF)
            for s, (a, b) in enumerate(KS):
                split_lo(s, r + 2, (b - a) * 2 * P)

            def c_pair(j, more):
                if more:
                    for s, (a, b) in enumerate(KS[:2]):
                        split_lo(s, j + (r + 3), (b - a) * 2 * P)
                for e in range(2):
                    dve.wait_ge(s_zl, 2 * j + (e + 1))
                    V.scalar_tensor_tensor(out=sp[e][:, :], in0=bank[e][:, 0:3 * P], scalar=0.0, in1=sp_abs[e][:, :],
                                           op0=ALU.max, op1=ALU.add).then_inc(s_sp, 1)
                if more:
                    split_lo(2, j + (r + 3), 2 * 2 * P)

            with dve.Fori(0, PAIRS_C - 1) as j:
                c_pair(j, True)
            c_pair(PAIRS_C - 1, False)
            r = R_C + 2 + PAIRS_C
            for s, (a, b) in enumerate(KS):
                split_lo(s, r, (b - a) * HALF)
            transposed_lo(T_C_O, None)
            for s, (a, b) in enumerate(KS):
                split_lo(s, r + 1, (b - a) * HALF)
            ffn(3, 1.0)

            residual(NORM_END, 0.5)
            means(NORM_END)
            dve.wait_ge(s_gf, 16)
            for t in range(NT):
                dve.wait_ge(s_rs, NT * NORM_END + t + 1)
                V.scalar_tensor_tensor(out=rows[:, t, :], in0=xres[:, t, :], scalar=rstd[:, t:t + 1], in1=g_fin[:, :],
                                       op0=ALU.mult, op1=ALU.mult).then_inc(s_y, 1)

        @block.tensor
        def _(pe):
            MM = nc.tensor.matmul
            pe.sem_inc(s_tq, 1)
            pe.sem_inc(s_on, 1)
            pe.sem_inc(s_oe, 1)

            def mm3(dst, a_hi, a_lo, b_hi, b_lo, start, stop):
                MM(dst, a_hi, b_hi, start=start, stop=False)
                MM(dst, a_hi, b_lo, start=False, stop=False)
                return MM(dst, a_lo, b_hi, start=False, stop=stop)

            def transposes(k, ready):
                for t in range(NT):
                    ready(t)
                    for i in range(KT):
                        end = nc.tensor.transpose(bank[i // 2][:, (i % 2) * SEQ + t * P:(i % 2) * SEQ + (t + 1) * P],
                                                  rows[:, t, i * P:(i + 1) * P], ident)
                    end.then_inc(s_xt, 1)

            T = (t_hi, t_lo)

            def by_slot(slot, r, tiles, lhs, n, dst, first, last, tile_done=None):
                pe.wait_ge(s_lo[slot], r + 1)
                for t in range(NT):
                    outs = dst(t)
                    for i, k in enumerate(tiles):
                        hi, lo = (x[:, k, t * P:(t + 1) * P] for x in lhs)
                        for m, o in enumerate(outs):
                            c = (i * len(outs) + m) * n
                            end = mm3(o, hi, lo, w_hi[slot][:, c:c + n], w_lo[slot][:, c:c + n],
                                      first and i == 0, last and i == len(tiles) - 1)
                    if t == 0 and tile_done is not None:
                        end.then_inc(tile_done, 1)
                end.then_inc(s_used[slot], 1)

            def block_round(r, n, dst, tile_done=None):
                for s, (a, b) in enumerate(KS):
                    by_slot(s, r, range(a, b), T, n, dst, s == 0, s == 2, tile_done if s == 2 else None)

            def ffn(f):
                r0, b = R_FFN[f], f * NCH
                n = NORM_FFN[f]
                transposes(T_FFN[f], lambda t: pe.wait_ge(s_xn, NT * n + t + 1))

                def up(c, slot):
                    by_slot(slot, c + r0, range(4 * slot, 4 * slot + 4), T, 2 * CH, lambda t: [bank[t][:, :]],
                            slot == 0, slot == 1, s_gu if slot == 1 else None)

                def turn(c):
                    for t in range(NT):
                        pe.wait_ge(s_h, (c + b) * NT + (t + 1))
                        for k in range(FT):
                            end = nc.tensor.transpose(bank[2][:, k * SEQ + t * P:k * SEQ + (t + 1) * P],
                                                      hid[:, t, k * P:(k + 1) * P], ident)
                    end.then_inc(s_ht, 1)

                def down(c, first, last):
                    pe.wait_ge(s_hl, c + (b + 1))
                    by_slot(2, c + r0, range(FT), (h_hi, h_lo), HALF, lambda t: [acc[t][h][:, :] for h in range(2)],
                            first, last, s_acc if last else None)

                pe.wait_ge(s_tl, KT * (T_FFN[f] + 1))
                up(0, 0)
                up(0, 1)
                turn(0)
                up(1, 0)
                up(1, 1)
                down(0, True, False)
                with pe.Fori(2, NCH) as c:
                    turn(c - 1)
                    up(c, 0)
                    up(c, 1)
                    down(c - 1, False, False)
                turn(NCH - 1)
                down(NCH - 1, False, True)

            pe.wait_ge(s_tab, 32)
            pe.wait_ge(s_gr, 8 * 16)
            nc.tensor.transpose(bank[7][:, 0:N_G], g_rows[0:N_G, :], ident[0:N_G, 0:N_G]).then_inc(s_gt, 1)
            ffn(0)

            r = R_AB
            transposes(T_AB, lambda t: pe.wait_ge(s_xn, NT * NORM_AB + t + 1))
            pe.wait_ge(s_tl, KT * (T_AB + 1))
            block_round(r, LAT, lambda t: [bank[t][:, 0:LAT]])
            block_round(r + 1, H_A * DH, lambda t: [bank[4 + t][:, :]])
            pe.wait_ge(s_ln, 4)
            for t in range(NT):
                for i in range(3):
                    end = nc.tensor.transpose(bank[2 + i // 2][:, (i % 2) * SEQ + t * P:(i % 2) * SEQ + (t + 1) * P],
                                              lat[:, t, i * P:(i + 1) * P], ident)
            end.then_inc(s_lt, 1)
            pe.wait_ge(s_ltl, 3)
            pe.wait_ge(s_vc, NT)
            LT = (lt_hi, lt_lo)
            q_banks = lambda t: [bank[(6, 4)[t] + i][:, 0:4 * QD] for i in range(2)]
            by_slot(0, r + 2, [0], LT, 4 * QD, q_banks, True, False)
            by_slot(1, r + 2, [1], LT, 4 * QD, q_banks, False, True)
            by_slot(2, r + 2, [2], LT, 4 * 2 * DH, lambda t: [bank[2 * t + i][:, :] for i in range(2)], True, True)

            def project_qk(slot, r, bk):
                a, b = KS[slot]
                pe.wait_ge(s_lo[slot], r + 1)
                for k in range(a, b):
                    for i in range(2):
                        c = ((k - a) * 2 + i) * P
                        dst = bk[:, i * SEQ:(i + 1) * SEQ]
                        hi, lo = w_hi[slot][:, c:c + P], w_lo[slot][:, c:c + P]
                        MM(dst, hi, t_hi[:, k, :], start=k == 0 and i == 0, stop=False, skip_group_check=True)
                        MM(dst, hi, t_lo[:, k, :], start=False, stop=False, skip_group_check=True)
                        end = MM(dst, lo, t_hi[:, k, :], start=False, stop=k == KT - 1 and i == 1, skip_group_check=True)
                end.then_inc(s_used[slot], 1)

            pe.wait_ge(s_qb, 2 + 4)
            for s in range(3):
                project_qk(s, r + 3, bank[4])
            pe.wait_ge(s_kb, 4)
            pe.wait_ge(s_vb, 4)

            def scores_a(j):
                pe.wait_ge(s_qkc, 2 * j + 2)
                for e in range(2):
                    q, k = (qk_t[e * DH:(e + 1) * DH, i * SEQ:(i + 1) * SEQ] for i in range(2))
                    MM(bank[e][:, 0:3 * P], tabb[:, bass.ds(j * (2 * P) + (BC["slopes"][0] + e * P), P)], tb("dist"), start=True, stop=False, skip_group_check=True)
                    MM(bank[e][:, 0:P], q[:, 0:P], k[:, 0:P], start=False, stop=False, skip_group_check=True)
                    MM(bank[e][:, P:3 * P], q[:, P:SEQ], k, start=False, stop=True, skip_group_check=True).then_inc(s_sc, 1)

            def scores_b():
                for e in range(2):
                    q, k = (qk_b[e][0:QD, i * SEQ:(i + 1) * SEQ] for i in range(2))
                    MM(bank[e][:, 0:3 * P], tb("identb"), tb("causal"), start=True, stop=False, skip_group_check=True)
                    MM(bank[e][:, 0:P], q[:, 0:P], k[:, 0:P], start=False, stop=False, skip_group_check=True)
                    MM(bank[e][:, P:3 * P], q[:, P:SEQ], k, start=False, stop=True, skip_group_check=True).then_inc(s_sc, 1)

            def turn_probs(src, e):
                for i in range(3):
                    end = nc.tensor.transpose(bank[2 + e][:, i * P:(i + 1) * P], src[e][:, i * P:(i + 1) * P], ident)
                end.then_inc(s_pt, 1)

            def weigh(n, v, col):
                pe.wait_ge(s_pe[0], n + 1)
                pe.wait_ge(s_pe[1], n + 1)
                pe.wait_ge(s_on, n + 1)
                for t in range(NT):
                    for e in range(2):
                        w = DH + 1
                        dst = bank[7][:, (2 * t + e) * w:(2 * t + e + 1) * w]
                        for i in range(t + 1):
                            end = MM(dst, pt[e][:, (t + i) * P:(t + i + 1) * P], v[:, i, bass.ds(col + e * w, w)],
                                     start=t == 0 and e == 0, stop=t == 1 and e == 1 and i == 1, skip_group_check=True)
                end.then_inc(s_pv, 1)

            def ab_pair(j, more):
                scores_a(j)
                pe.wait_ge(s_st, 2 * j + 2)
                for e in range(2):
                    for i, st in enumerate((q_st, k_st)):
                        for t in range(NT):
                            end = nc.tensor.transpose(bank[5 + e][0:QD, i * SEQ + t * P:i * SEQ + (t + 1) * P],
                                                      st[:, t, e * QD:(e + 1) * QD], ident)
                end.then_inc(s_tq, 1)
                if more:
                    project_qk(0, j + (r + 4), bank[4])
                for e in range(2):
                    pe.wait_ge(s_cn, 2 * j + (e + 1))
                    turn_probs(pc, e)
                for e in range(2):
                    pe.wait_ge(s_qbt[e], j + 1)
                scores_b()
                if more:
                    project_qk(1, j + (r + 4), bank[4])
                weigh(2 * j, v_a, j * (2 * (DH + 1)))
                for e in range(2):
                    pe.wait_ge(s_ex, 4 * j + (e + 3))
                    turn_probs(pr, e)
                if more:
                    project_qk(2, j + (r + 4), bank[4])
                weigh(2 * j + 1, v_b, j * (2 * (DH + 1)))

            with pe.Fori(0, PAIRS_A - 1) as j:
                ab_pair(j, True)
            ab_pair(PAIRS_A - 1, False)

            def project_out(r):
                block_round(r, HALF, lambda t: [acc[t][0][:, :]])
                block_round(r + 1, HALF, lambda t: [acc[t][1][:, :]], s_acc)

            transposes(T_AB_O, lambda t: pe.wait_ge(s_on, 1 + 2 * PAIRS_A))
            pe.wait_ge(s_tl, KT * (T_AB_O + 1))
            project_out(R_AB + 3 + PAIRS_A)
            ffn(1)
            ffn(2)

            r = R_C
            transposes(T_C, lambda t: pe.wait_ge(s_xn, NT * NORM_C + t + 1))
            pe.wait_ge(s_tl, KT * (T_C + 1))
            block_round(r, HALF, lambda t: [bank[t][:, :]])
            block_round(r + 1, HALF, lambda t: [bank[2 + t][:, :]])
            for s in range(3):
                project_qk(s, r + 2, bank[4])
            pe.wait_ge(s_vc, 3 * NT)

            def c_pair(j, more):
                pe.wait_ge(s_qkc, 2 * j + (2 * PAIRS_A + 2))
                for e in range(2):
                    q, k = (qk_t[e * DH:(e + 1) * DH, i * SEQ:(i + 1) * SEQ] for i in range(2))
                    MM(bank[e][:, 0:3 * P], tb("identb"), tb("strict"), start=True, stop=False, skip_group_check=True)
                    MM(bank[e][:, 0:SEQ], k[:, 0:P], q, start=False, stop=False, skip_group_check=True)
                    MM(bank[e][:, SEQ:3 * P], k[:, P:SEQ], q[:, P:SEQ], start=False, stop=True,
                       skip_group_check=True).then_inc(s_z, 1)
                if more:
                    project_qk(0, j + (r + 3), bank[4])
                    project_qk(1, j + (r + 3), bank[4])
                for e in range(2):
                    pe.wait_ge(s_sp, 2 * j + (e + 1))
                    MM(bank[e][:, 0:3 * P], tf("neg_tri"), sp[e][:, :], start=False, stop=False, skip_group_check=True)
                    MM(bank[e][:, P:SEQ], tf("neg_one"), sp[e][:, SEQ:], start=False, stop=True,
                       skip_group_check=True).then_inc(s_cs, 1)
                if more:
                    project_qk(2, j + (r + 3), bank[4])
                pe.wait_ge(s_oe, j + 1)
                for e in range(2):
                    pe.wait_ge(s_at, 2 * j + (e + 1))
                    for t in range(NT):
                        dst = bank[3][:, (2 * t + e) * DH:(2 * t + e + 1) * DH]
                        for i in range(t + 1):
                            c = (t + i) * P
                            end = MM(dst, pr[e][:, c:c + P], v_c[:, i, bass.ds(j * P + e * DH, DH)],
                                     start=t == 0 and e == 0, stop=e == 1 and t == 1 and i == 1, skip_group_check=True)
                end.then_inc(s_oc, 1)

            with pe.Fori(0, PAIRS_C - 1) as j:
                c_pair(j, True)
            c_pair(PAIRS_C - 1, False)
            transposes(T_C_O, lambda t: pe.wait_ge(s_oe, 1 + PAIRS_C))
            pe.wait_ge(s_tl, KT * (T_C_O + 1))
            project_out(R_C + 2 + PAIRS_C)
            ffn(3)


_INS = ["x", "ffn_norm_g", "mix_norm_g", "ffn_w_gate", "ffn_w_up", "ffn_w_down", "ab_w_in", "mla_q_norm_g",
        "mla_w_uq", "mla_kv_norm_g", "mla_w_ukv", "ab_w_out", "sb_w_in", "sb_w_out", "final_norm_g"]


def tables(np):
    f, nf, b, nb = layout(1024, 2816, 256)
    tf, tb = np.zeros((P, nf), np.float32), np.zeros((P, nb), np.float32)
    row, col = np.arange(P)[:, None], np.arange(P)[None, :]

    def put(t, at, name, values):
        t[:, at[name][0]:at[name][1]] = np.asarray(values, np.float32).reshape(P, -1)

    put(tf, f, "ident", row == col)
    put(tf, f, "neg_tri", -1.0 * (row >= col))
    put(tf, f, "neg_one", -np.ones((P, P)))
    dist = np.concatenate([row - col, row - col + P, row - col], axis=1)
    count = (dist >= 0) * ((dist <= 128) * 1 + (dist % 4 == 0) + (dist % 16 == 0))
    put(tf, f, "count", count)
    put(tb, b, "dist", np.where(count > 0, -dist, NEG))
    put(tb, b, "causal", np.where(dist >= 0, 0.0, NEG))
    put(tb, b, "identb", row == col)
    put(tb, b, "slopes", np.concatenate([2.0 ** -(h + 1) * (row == col) for h in range(8)], axis=1))
    strict = np.where(row < col, 0.0, NEG)
    put(tb, b, "strict", np.concatenate([strict, np.zeros((P, P)), strict], axis=1))
    inv = np.float32(10000.0) ** (-np.arange(0, 32, 2, dtype=np.float32) / np.float32(32))
    ang = np.arange(256, dtype=np.float32)[:, None] * inv[None, :].astype(np.float32)
    for name, fn in (("cos", np.cos), ("sin", np.sin)):
        put(tf, f, name, np.repeat(fn(ang).reshape(2, P, 1, 16).transpose(1, 0, 2, 3), 9, axis=2))
    return tf, (tb.view(np.uint32) >> 16).astype(np.uint16)


def kernel(**inputs):
    import numpy as np
    import concourse.bacc as bacc
    from concourse.bass_utils import run_bass_kernel_spmd

    nc = bacc.Bacc("TRN2", target_bir_lowering=False, num_devices=1)
    arrays, args = {}, []
    table_f, table_b = tables(np)
    for name, a in [(n, inputs[n]) for n in _INS] + [("table_f", table_f), ("table_b", table_b)]:
        a = np.ascontiguousarray(a)
        arrays[f"in_{name}_dram"] = a
        args.append(nc.dram_tensor(f"in_{name}_dram", a.shape, mybir.dt.from_np(a.dtype), kind="ExternalInput").ap())
    shape = tuple(inputs["x"].shape)
    out = nc.dram_tensor("out_0_dram", shape, mybir.dt.float32, kind="ExternalOutput").ap()
    trunk_kernel(nc, *args, out)
    r = run_bass_kernel_spmd(nc, [arrays], core_ids=[0])
    return r.results[0]["out_0_dram"]
```

```python
import concourse.bass as bass
from concourse import mybir
from contextlib import ExitStack


P = 128
NEG = -1e30


def layout(D, F, SEQ):
    f, b, at_f, at_b = {}, {}, 0, 0
    for name, n in (("ident", P), ("neg_tri", P), ("neg_one", P), ("count", 3 * P),
                    ("cos", 2 * 9 * 16), ("sin", 2 * 9 * 16)):
        f[name] = (at_f, at_f + n)
        at_f += n
    for name, n in (("identb", P), ("slopes", 8 * P), ("dist", 3 * P), ("causal", 3 * P), ("strict", 3 * P)):
        b[name] = (at_b, at_b + n)
        at_b += n
    return f, at_f, b, at_b


def trunk_kernel(nc, x, ffn_norm_g, mix_norm_g, w_gate, w_up, w_down, ab_w_in, q_norm_g, w_uq, kv_norm_g,
                 w_ukv, ab_w_out, sb_w_in, sb_w_out, final_norm_g, table_f, table_b, out):
    fp32, f32r, bf16, u16 = mybir.dt.float32, mybir.dt.float32r, mybir.dt.bfloat16, mybir.dt.uint16
    ALU, ACT, AX = mybir.AluOpType, mybir.ActivationFunctionType, mybir.AxisListType

    _, SEQ, D = x.shape
    F = w_gate.shape[-1]
    EPS = 1e-6
    NT = SEQ // P
    KT = D // P
    HALF = D // 2
    CH = 256
    NCH = F // CH
    FT = CH // P
    KS = ((0, 3), (3, 6), (6, 8))
    DH = 64
    H_A, H_B, H_C = 8, 8, 16
    QD, ROPE = 96, 32
    RQ, RKV = q_norm_g.shape[-1], kv_norm_g.shape[-1]
    LAT = RQ + RKV + ROPE
    A_QKV = 3 * H_A * DH
    PAIRS_A, PAIRS_C = H_A // 2, H_C // 2
    G_Q = 6 * KT
    G_KV = G_Q + RQ // P
    N_G = G_KV + RKV // P

    ctx = ExitStack()
    with ctx:
        def sb(name, shape, dt=fp32):
            return ctx.enter_context(nc.sbuf_tensor(name, shape, dt))

        def sem(name):
            return ctx.enter_context(nc.semaphore(name))

        raw = [sb(f"raw{s}", [P, 2048]) for s in range(3)]
        w_hi = [sb(f"w_hi{s}", [P, 2048], f32r) for s in range(3)]
        w_lo = [sb(f"w_lo{s}", [P, 2048], f32r) for s in range(3)]
        xres = sb("xres", [P, NT, D])
        rows = sb("rows", [P, NT, D])
        t_hi = sb("t_hi", [P, KT, SEQ], f32r)
        t_lo = sb("t_lo", [P, KT, SEQ], f32r)
        junk = sb("junk", [P, D])
        hid = sb("hid", [P, NT, CH])
        gate = sb("gate", [P, NT, CH])
        h_hi = sb("h_hi", [P, FT, SEQ], f32r)
        h_lo = sb("h_lo", [P, FT, SEQ], f32r)
        ss = sb("ss", [P, NT])
        ms = sb("ms", [P, NT])
        rstd = sb("rstd", [P, NT])
        r_sq = sb("r_sq", [P, NT, P])
        r_row = sb("r_row", [P, 2 * SEQ])
        half_neg = sb("half_neg", [P, 4])
        g_rows = sb("g_rows", [P, P])
        g_col = sb("g_col", [P, P])
        g_fin = sb("g_fin", [P, D])
        FC, nf, BC, nb = layout(D, F, SEQ)
        tabf = sb("tabf", [P, nf])
        tabb = sb("tabb", [P, nb], bf16)
        qk_t = sb("qk_t", [P, 2 * SEQ])
        pr = [sb(f"pr{e}", [P, 3 * P]) for e in range(2)]
        pc = [sb(f"pc{e}", [P, 3 * P]) for e in range(2)]
        pt = [sb(f"pt{e}", [P, 3 * P]) for e in range(2)]
        nmax = sb("nmax", [P, 2, NT])
        rden = sb("rden", [P, NT, 2, 1])
        v_a = sb("v_a", [P, NT, H_A * (DH + 1)])
        v_b = sb("v_b", [P, NT, H_B * (DH + 1)])
        v_c = sb("v_c", [P, NT, H_C * DH])
        lat = sb("lat", [P, NT, RQ + RKV])
        lat_ss = sb("lat_ss", [P, NT, 2])
        lat_ms = sb("lat_ms", [P, NT, 2])
        lat_rstd = sb("lat_rstd", [P, NT, 2])
        lt_hi = sb("lt_hi", [P, 3, SEQ], f32r)
        lt_lo = sb("lt_lo", [P, 3, SEQ], f32r)
        q_b = sb("q_b", [P, NT, 9 * QD])
        k_b = sb("k_b", [P, NT, H_B * QD])
        rot = [sb(f"rot{i}", [P, NT, 9, 16]) for i in range(4)]
        q_st = sb("q_st", [P, NT, 2 * QD])
        k_st = sb("k_st", [P, NT, 2 * QD])
        qk_b = [sb(f"qk_b{e}", [P, 2 * SEQ]) for e in range(2)]
        sp_abs = [sb(f"sp_abs{e}", [P, 3 * P]) for e in range(2)]
        sp_exp = [sb(f"sp_exp{e}", [P, 3 * P]) for e in range(2)]
        sp = [sb(f"sp{e}", [P, 3 * P]) for e in range(2)]

        bank = [ctx.enter_context(nc.psum_tensor(f"bank{i}", [P, 512], fp32)) for i in range(8)]
        acc = [[bank[4 + 2 * t + h] for h in range(2)] for t in range(NT)]

        def tf(name):
            return tabf[:, FC[name][0]:FC[name][1]]

        def tb(name, lo=0, hi=None):
            a, b = BC[name]
            return tabb[:, a + lo:(b if hi is None else a + hi)]

        ident = tf("ident")

        s_in = [sem(f"x_loaded{t}") for t in range(NT)]
        s_id = sem("identity_loaded")
        s_tab = sem("tables_loaded")
        s_gr = sem("gain_rows_loaded")
        s_gf = sem("final_gain_loaded")
        s_raw = [sem(f"raw_loaded{s}") for s in range(3)]
        s_hi = [sem(f"high_ready{s}") for s in range(3)]
        s_lo = [sem(f"low_ready{s}") for s in range(3)]
        s_used = [sem(f"weights_used{s}") for s in range(3)]
        s_half = sem("constants_set")
        s_gt = sem("gains_transposed")
        s_gc = sem("gains_ready")
        s_acc = sem("sublayer_summed")
        s_x = sem("residual_updated")
        s_ss = sem("squares_summed")
        s_ms = sem("mean_square_ready")
        s_rs = sem("rstd_ready")
        s_rb = sem("rstd_repeated")
        s_rr = sem("rstd_transposed")
        s_rc = sem("rstd_rows_ready")
        s_xt = sem("rows_transposed")
        s_th = sem("transpose_high_ready")
        s_tl = sem("transpose_low_ready")
        s_gu = sem("gate_up_summed")
        s_sg = sem("silu_ready")
        s_h = sem("hidden_ready")
        s_ht = sem("hidden_transposed")
        s_hh = sem("hidden_high_ready")
        s_hl = sem("hidden_low_ready")
        s_vc = sem("v_copied")
        s_qkc = sem("qk_copied")
        s_lss = sem("latent_squares_summed")
        s_lms = sem("latent_mean_square_ready")
        s_lrs = sem("latent_rstd_ready")
        s_ln = sem("latents_normed")
        s_lt = sem("latents_transposed")
        s_lth = sem("latent_high_ready")
        s_ltl = sem("latent_low_ready")
        s_qb = sem("mla_q_copied")
        s_kb = sem("mla_k_copied")
        s_vb = sem("mla_v_copied")
        s_rt = sem("rotary_products_ready")
        s_ro = sem("rotary_applied")
        s_kr = sem("mla_k_complete")
        s_st = sem("mla_pair_staged")
        s_tq = sem("mla_pair_transposed")
        s_qbt = [sem(f"mla_head_ready{e}") for e in range(2)]
        s_sc = sem("scores_ready")
        s_mx = sem("max_ready")
        s_ex = sem("exp_ready")
        s_cn = sem("counted")
        s_pt = sem("probs_transposed")
        s_pe = [sem(f"probs_copied{e}") for e in range(2)]
        s_pv = sem("pv_summed")
        s_rd = sem("denominators_inverted")
        s_on = sem("outputs_normed")
        s_z = sem("z_ready")
        s_za = sem("z_abs_ready")
        s_ze = sem("z_exp_ready")
        s_zl = sem("z_log_ready")
        s_sp = sem("softplus_ready")
        s_cs = sem("logits_ready")
        s_at = sem("weights_ready")
        s_oc = sem("stick_summed")
        s_oe = sem("stick_copied")
        s_y = sem("final_rows_ready")
        s_out = sem("stored")

        block = ctx.enter_context(nc.Block())

        FFN_ROUNDS = (NCH, NCH + 1, NCH - 1)
        A_ROUNDS, C_ROUNDS = (3 + PAIRS_A + 2,) * 3, (2 + PAIRS_C + 2,) * 3
        R_NORM = [(0, 0, 0)]
        for rounds in (FFN_ROUNDS, A_ROUNDS, FFN_ROUNDS, FFN_ROUNDS, C_ROUNDS, FFN_ROUNDS):
            R_NORM.append(tuple(a + b for a, b in zip(R_NORM[-1], rounds)))
        NORM_FFN, NORM_AB, NORM_C, NORM_END = [0, 2, 3, 5], 1, 4, 6
        R_FFN, R_AB, R_C = [R_NORM[n] for n in NORM_FFN], R_NORM[NORM_AB], R_NORM[NORM_C]
        LAST_SLOT = [1 if n in NORM_FFN else 2 for n in range(NORM_END)]
        T_FFN, T_AB, T_AB_O, T_C, T_C_O = [0, 3, 4, 7], 1, 2, 5, 6
        T_BANKS = {k: (0, 1, 2, 3) if k in (T_AB_O, T_C_O) else (2, 3, 4, 5) for k in range(8)}

        @block.sync
        def _(sp_):
            def load(slot, r, parts):
                if not (isinstance(r, int) and r == 0):
                    sp_.wait_ge(s_lo[slot], r)
                for dst, src in parts:
                    sp_.dma_start(dst, src).then_inc(s_raw[slot], 16)

            def load_up(f, c, slot):
                kt = slice(4 * slot, 4 * slot + 4)
                dst = raw[slot][:, :].rearrange("p (k b n) -> p k b n", k=4, b=2)
                load(slot, c + R_FFN[f][slot], [
                    (dst[:, :, b, :], w[f // 2, f % 2].rearrange("(k p) n -> p k n", p=P)[:, kt, bass.ds(c * CH, CH)])
                    for b, w in ((0, w_gate), (1, w_up))])

            def load_down(f, c, slot, r):
                src = w_down[f // 2, f % 2]
                load(slot, c + r, [
                    (raw[slot][:, i * D:(i + 1) * D], src[bass.ds(c * CH + i * P, P), :]) for i in range(FT)])

            def load_ffn(f):
                if f:
                    for s in range(2):
                        load_up(f, 0, s)
                with sp_.Fori(1, NCH) as c:
                    for s in range(2):
                        load_up(f, c, s)
                    load_down(f, c - 1, 2, R_FFN[f][2])
                load_down(f, NCH - 1, 1, R_FFN[f][1] + 1)

            def load_block(w, R, r, col, n):
                src = w.rearrange("(k p) n -> p k n", p=P)
                for s, (a, b) in enumerate(KS):
                    dst = raw[s][:, 0:(b - a) * n].rearrange("p (k n) -> p k n", k=b - a)
                    load(s, R[s] + r, [(dst[:, 0:1, :], src[:, a:a + 1, bass.ds(col, n)]),
                                (dst[:, 1:, :], src[:, a + 1:b, bass.ds(col, n)])])

            def load_qk(w, R, r, j, width):
                src = w.rearrange("(k p) n -> p k n", p=P)
                for s, (a, b) in enumerate(KS):
                    dst = raw[s][:, 0:(b - a) * 2 * P].rearrange("p (k b n) -> p k b n", k=b - a, b=2)
                    load(s, R[s] + r, [(dst[:, :, i, :], src[:, a:b, bass.ds(j * P + i * width, P)]) for i in range(2)])

            load_up(0, 0, 0)
            load_up(0, 0, 1)
            sp_.dma_start(tabb[:, :].bitcast(u16), table_b).then_inc(s_tab, 16)
            sp_.dma_start(tabf[:, P:], table_f[:, P:]).then_inc(s_tab, 16)
            sp_.dma_start(g_fin[:, :], final_norm_g.partition_broadcast(P)).then_inc(s_gf, 16)

            load_ffn(0)
            load_block(ab_w_in[0], R_AB, 0, A_QKV, LAT)
            load_block(ab_w_in[0], R_AB, 1, 2 * H_A * DH, H_A * DH)
            for s in range(RQ // P):
                n = H_B * QD // 2
                load(s, R_AB[s] + 2, [(raw[s][:, i * n:(i + 1) * n], w_uq[0, s * P:(s + 1) * P, i * n:(i + 1) * n])
                                      for i in range(2)])
            n = H_B * 2 * DH // 2
            load(2, R_AB[2] + 2, [(raw[2][:, i * n:(i + 1) * n], w_ukv[0, :, i * n:(i + 1) * n]) for i in range(2)])
            with sp_.Fori(0, PAIRS_A) as j:
                load_qk(ab_w_in[0], R_AB, 3 + j, j, H_A * DH)
            with sp_.Fori(0, 2) as j:
                load_block(ab_w_out[0], R_AB, 3 + PAIRS_A + j, j * HALF, HALF)
            load_ffn(1)
            load_ffn(2)
            with sp_.Fori(0, 2) as j:
                load_block(sb_w_in[0], R_C, j, 2 * D + j * HALF, HALF)
            with sp_.Fori(0, PAIRS_C) as j:
                load_qk(sb_w_in[0], R_C, 2 + j, j, D)
            with sp_.Fori(0, 2) as j:
                load_block(sb_w_out[0], R_C, 2 + PAIRS_C + j, j * HALF, HALF)
            load_ffn(3)
            for t in range(NT):
                sp_.wait_ge(s_y, t + 1)
                sp_.dma_start(out[0, t * P:(t + 1) * P, :], rows[:, t, :]).then_inc(s_out, 16)
            sp_.wait_ge(s_out, 16 * NT)

        @block.gpsimd
        def _(pool):
            nc.gpsimd.memset(half_neg[:, :], -0.5).then_inc(s_half, 1)
            nc.gpsimd.memset(v_a[:, :, :], 1.0).then_inc(s_half, 1)
            nc.gpsimd.memset(v_b[:, :, :], 1.0).then_inc(s_half, 1)
            pool.wait_ge(s_half, 3)

            def root(n):
                pool.wait_ge(s_ms, n + 1)
                nc.gpsimd.tensor_tensor(rstd[:, :], ms[:, :], half_neg[:, 0:NT], ALU.pow).then_inc(s_rs, 1)

            root(NORM_FFN[0])
            root(NORM_AB)
            pool.wait_ge(s_lms, 2)
            nc.gpsimd.tensor_tensor(lat_rstd[:, :, :].rearrange("p t n -> p (t n)"),
                                    lat_ms[:, :, :].rearrange("p t n -> p (t n)"), half_neg[:, :], ALU.pow).then_inc(s_lrs, 1)
            pool.wait_ge(s_tab, 32)
            pool.wait_ge(s_ro, 2)
            pool.wait_ge(s_kr, 1)
            with pool.Fori(0, PAIRS_A) as j:
                pool.wait_ge(s_tq, j + 1)
                nc.gpsimd.tensor_copy(q_st[:, :, :], q_b[:, :, bass.ds(j * (2 * QD), 2 * QD)]).then_inc(s_st, 1)
                nc.gpsimd.tensor_copy(k_st[:, :, :], k_b[:, :, bass.ds(j * (2 * QD), 2 * QD)]).then_inc(s_st, 1)
                for e in range(2):
                    pool.wait_ge(s_ex, j * 4 + (e + 1))
                    nc.gpsimd.tensor_tensor(pc[e][:, :], pr[e][:, :], tf("count"), ALU.mult).then_inc(s_cn, 1)
            for n in (2, 3, 4, 5, 6):
                root(n)

        @block.scalar
        def _(act):
            A = nc.scalar.activation

            def split_hi(slot, r, n):
                act.wait_ge(s_raw[slot], r * 32 + 32)
                if not (isinstance(r, int) and r == 0):
                    act.wait_ge(s_used[slot], r)
                A(w_hi[slot][:, 0:n], raw[slot][:, 0:n], ACT.Copy).then_inc(s_hi[slot], 1)

            def squares(n):
                for t in range(NT):
                    if n == 0:
                        act.wait_ge(s_in[t], 16)
                    else:
                        act.wait_ge(s_x, 4 * (n - 1) + 2 * t + 2)
                    if NT * n + t:
                        act.wait_ge(s_ss, NT * n + t)
                    if n == NORM_AB + 1:
                        act.wait_ge(s_lss, 4)
                    A(junk[:, :], xres[:, t, :], ACT.Square, accum_out=ss[:, t:t + 1]).then_inc(s_ss, 1)

            def transposed_hi(k, g0):
                for i in range(KT):
                    if i % 4 == 0:
                        act.wait_ge(s_xt, 2 * k + i // 4 + 1)
                    if k + i == 0:
                        act.wait_ge(s_gc, 1)
                    src = bank[T_BANKS[k][i // 2]][:, (i % 2) * SEQ:(i % 2 + 1) * SEQ]
                    scale = 1.0 if g0 is None else g_col[:, g0 + i:g0 + i + 1]
                    A(t_hi[:, i, :], src, ACT.Copy, scale=scale).then_inc(s_th, 1)

            def rstd_rows(n):
                act.wait_ge(s_rr, n)
                A(r_row[:, 0:SEQ], bank[7][:, 0:SEQ], ACT.Copy, scale=DH ** -0.5).then_inc(s_rc, 1)
                A(r_row[:, SEQ:], bank[7][:, 0:SEQ], ACT.Copy).then_inc(s_rc, 1)

            def ffn(f):
                r0, b = R_FFN[f], f * NCH
                act.preload_act_table(ACT.Silu)
                split_hi(0, r0[0], 2048)
                transposed_hi(T_FFN[f], f * KT)
                split_hi(1, r0[1], 2048)
                squares(NORM_FFN[f])
                act.wait_ge(s_rs, NORM_FFN[f] + 1)

                def silu(c):
                    for t in range(NT):
                        if t == 0:
                            act.wait_ge(s_gu, c + (b + 1))
                        else:
                            act.wait_ge(s_used[1], c + (r0[1] + 1))
                        A(gate[:, t, :], bank[t][:, 0:CH], ACT.Silu, scale=rstd[:, t:t + 1]).then_inc(s_sg, 1)

                def hidden_hi(c):
                    act.wait_ge(s_ht, c + (b + 1))
                    A(h_hi[:, :, :].rearrange("p k n -> p (k n)"), bank[2][:, :], ACT.Copy).then_inc(s_hh, 1)

                with act.Fori(1, NCH) as c:
                    split_hi(0, c + r0[0], 2048)
                    silu(c - 1)
                    split_hi(1, c + r0[1], 2048)
                    hidden_hi(c - 1)
                    split_hi(2, c + (r0[2] - 1), 2048)
                silu(NCH - 1)
                split_hi(1, r0[1] + NCH, 2048)
                hidden_hi(NCH - 1)

            act.dma_start(tabf[:, 0:P], table_f[:, 0:P]).then_inc(s_id, 16)
            for t in range(NT):
                act.dma_start(xres[:, t, :], x[0, t * P:(t + 1) * P, :]).then_inc(s_in[t], 16)
            for a, src in ((0, ffn_norm_g.rearrange("l s (k p) -> (l s k) p", p=P)),
                           (4 * KT, mix_norm_g.rearrange("l (k p) -> (l k) p", p=P)),
                           (G_Q, q_norm_g.rearrange("l (k p) -> (l k) p", p=P)),
                           (G_KV, kv_norm_g.rearrange("l (k p) -> (l k) p", p=P))):
                act.dma_start(g_rows[a:a + src.shape[0], :], src).then_inc(s_gr, 16)
            act.wait_ge(s_gt, 1)
            A(g_col[:, 0:N_G], bank[7][:, 0:N_G], ACT.Copy).then_inc(s_gc, 1)
            ffn(0)

            r = R_AB
            split_hi(0, r[0], 3 * LAT)
            split_hi(2, r[2], 2 * LAT)
            transposed_hi(T_AB, 4 * KT)
            split_hi(1, r[1], 3 * LAT)
            squares(NORM_AB)
            for s, (a, b) in enumerate(KS):
                split_hi(s, r[s] + 1, (b - a) * H_A * DH)
            rstd_rows(1)
            act.wait_ge(s_used[2], r[2] + 1)
            for t in range(NT):
                for i, (a, n) in enumerate(((0, RQ), (RQ, RKV))):
                    act.wait_ge(s_ss, 2 * NT) if t + i == 0 else act.wait_ge(s_lss, 2 * t + i)
                    A(junk[:, 0:n], bank[t][:, a:a + n], ACT.Square, scale=rstd[:, t:t + 1],
                      accum_out=lat_ss[:, t, i:i + 1]).then_inc(s_lss, 1)
            for t in range(NT):
                A(q_b[:, t, 8 * QD + DH:9 * QD], bank[t][:, RQ + RKV:LAT], ACT.Copy, scale=rstd[:, t:t + 1]).then_inc(s_qb, 1)
            act.wait_ge(s_lt, 1)
            for i in range(3):
                A(lt_hi[:, i, :], bank[2 + i // 2][:, (i % 2) * SEQ:(i % 2 + 1) * SEQ], ACT.Copy,
                  scale=g_col[:, G_Q + i:G_Q + i + 1]).then_inc(s_lth, 1)
            for s, n in enumerate((H_B * QD, H_B * QD, H_B * 2 * DH)):
                split_hi(s, r[s] + 2, n)
            act.wait_ge(s_used[2], r[2] + 2)
            act.wait_ge(s_half, 3)
            for t in range(NT):
                A(v_a[:, t, :].rearrange("p (h d) -> p h d", d=DH + 1)[:, :, 0:DH],
                  bank[4 + t][:, :].rearrange("p (h d) -> p h d", d=DH), ACT.Copy, scale=rstd[:, t:t + 1]).then_inc(s_vc, 1)
            act.wait_ge(s_used[1], r[1] + 3)
            for t in range(NT):
                for i in range(2):
                    A(q_b[:, t, i * 4 * QD:(i + 1) * 4 * QD], bank[(6, 4)[t] + i][:, 0:4 * QD], ACT.Copy,
                      scale=float(QD) ** -0.5).then_inc(s_qb, 1)
            act.wait_ge(s_used[2], r[2] + 3)
            for t in range(NT):
                for i in range(2):
                    A(v_b[:, t, i * 4 * (DH + 1):(i + 1) * 4 * (DH + 1)].rearrange("p (h d) -> p h d", d=DH + 1)[:, :, 0:DH],
                      bank[2 * t + i][:, :].rearrange("p (h d) -> p h d", d=2 * DH)[:, :, DH:2 * DH],
                      ACT.Copy).then_inc(s_vb, 1)
            for s, (a, b) in enumerate(KS):
                split_hi(s, r[s] + 3, (b - a) * 2 * P)
            act.preload_act_table(ACT.Exp)

            def exps(n, e):
                act.wait_ge(s_mx, 2 * n + (e + 1))
                A(pr[e][:, 0:P], bank[e][:, 0:P], ACT.Exp, bias=nmax[:, e, 0:1])
                A(pr[e][:, P:], bank[e][:, P:3 * P], ACT.Exp, bias=nmax[:, e, 1:2]).then_inc(s_ex, 1)

            def ab_pair(j, more):
                if more:
                    split_hi(0, j + (r[0] + 4), 3 * 2 * P)
                for e in range(2):
                    exps(2 * j, e)
                act.wait_ge(s_tq, 2 + j)
                A(qk_b[0][0:QD, :], bank[5][0:QD, :], ACT.Copy).then_inc(s_qbt[0], 1)
                if more:
                    split_hi(1, j + (r[1] + 4), 3 * 2 * P)
                act.wait_ge(s_pt, 4 * j + 1)
                A(pt[0][:, :], bank[2][:, 0:3 * P], ACT.Copy).then_inc(s_pe[0], 1)
                for e in range(2):
                    exps(2 * j + 1, e)
                if more:
                    split_hi(2, j + (r[2] + 4), 2 * 2 * P)
                act.wait_ge(s_pt, 4 * j + 3)
                act.wait_ge(s_pv, 2 * j + 1)
                A(pt[0][:, :], bank[2][:, 0:3 * P], ACT.Copy).then_inc(s_pe[0], 1)

            with act.Fori(0, PAIRS_A - 1) as j:
                ab_pair(j, True)
            ab_pair(PAIRS_A - 1, False)
            for s, (a, b) in enumerate(KS):
                split_hi(s, r[s] + (3 + PAIRS_A), (b - a) * HALF)
            transposed_hi(T_AB_O, None)
            for s, (a, b) in enumerate(KS):
                split_hi(s, r[s] + (4 + PAIRS_A), (b - a) * HALF)

            ffn(1)
            ffn(2)

            r = R_C
            split_hi(0, r[0], 3 * HALF)
            split_hi(2, r[2], 2 * HALF)
            transposed_hi(T_C, 5 * KT)
            split_hi(1, r[1], 3 * HALF)
            squares(NORM_C)
            for s, (a, b) in enumerate(KS):
                split_hi(s, r[s] + 1, (b - a) * HALF)
            rstd_rows(2)
            for n in range(2):
                act.wait_ge(s_used[2], r[2] + n + 1)
                for t in range(NT):
                    A(v_c[:, t, n * HALF:(n + 1) * HALF], bank[2 * n + t][:, :], ACT.Copy, scale=rstd[:, t:t + 1]).then_inc(s_vc, 1)
                if n == 0:
                    for s, (a, b) in enumerate(KS):
                        split_hi(s, r[s] + 2, (b - a) * 2 * P)
            act.preload_act_table_set("natural_log_exp_and_others")

            def c_pair(j, more):
                n = 2 * j
                if more:
                    split_hi(0, j + (r[0] + 3), 3 * 2 * P)
                for e in range(2):
                    act.wait_ge(s_z, n + (e + 1))
                    A(sp_abs[e][:, :], bank[e][:, 0:3 * P], ACT.Abs).then_inc(s_za, 1)
                if more:
                    split_hi(1, j + (r[1] + 3), 3 * 2 * P)
                for e in range(2):
                    act.wait_ge(s_za, n + (e + 1))
                    A(sp_exp[e][:, :], sp_abs[e][:, :], ACT.Exp, scale=-1.0).then_inc(s_ze, 1)
                for e in range(2):
                    act.wait_ge(s_ze, n + (e + 1))
                    A(sp_abs[e][:, :], sp_exp[e][:, :], ACT.Ln, bias=1.0).then_inc(s_zl, 1)
                if more:
                    split_hi(2, j + (r[2] + 3), 2 * 2 * P)
                for e in range(2):
                    act.wait_ge(s_cs, n + (e + 1))
                    A(pr[e][:, :], bank[e][:, 0:3 * P], ACT.Exp).then_inc(s_at, 1)
                act.wait_ge(s_oc, j + 1)
                A(rows[:, :, bass.ds(j * P, P)], bank[3][:, 0:SEQ].rearrange("p (t n) -> p t n", t=NT),
                  ACT.Copy).then_inc(s_oe, 1)

            with act.Fori(0, PAIRS_C - 1) as j:
                c_pair(j, True)
            c_pair(PAIRS_C - 1, False)
            for s, (a, b) in enumerate(KS):
                split_hi(s, r[s] + (2 + PAIRS_C), (b - a) * HALF)
            transposed_hi(T_C_O, None)
            for s, (a, b) in enumerate(KS):
                split_hi(s, r[s] + (3 + PAIRS_C), (b - a) * HALF)
            ffn(3)
            squares(NORM_END)

        @block.vector
        def _(dve):
            V = nc.vector

            def split_lo(slot, r, n):
                dve.wait_ge(s_hi[slot], r + 1)
                V.tensor_tensor(w_lo[slot][:, 0:n], raw[slot][:, 0:n], w_hi[slot][:, 0:n].bitcast(fp32),
                                ALU.subtract).then_inc(s_lo[slot], 1)

            def residual(n, scale):
                for t in range(NT):
                    if t == 0:
                        dve.wait_ge(s_acc, n)
                    else:
                        slot = LAST_SLOT[n - 1]
                        dve.wait_ge(s_used[slot], R_NORM[n][slot])
                    for h in range(2):
                        xs = xres[:, t, h * HALF:(h + 1) * HALF]
                        V.scalar_tensor_tensor(out=xs, in0=acc[t][h][:, :], scalar=scale, in1=xs,
                                               op0=ALU.mult, op1=ALU.add).then_inc(s_x, 1)

            def means(n):
                dve.wait_ge(s_ss, NT * n + NT)
                V.tensor_scalar(ms[:, :], ss[:, :], 1.0 / D, EPS, op0=ALU.mult, op1=ALU.add).then_inc(s_ms, 1)

            def rstd_columns(n):
                dve.wait_ge(s_rs, n + 1)
                V.tensor_copy(r_sq[:, :, :], rstd[:, :].unsqueeze(2).to_broadcast([P, NT, P])).then_inc(s_rb, 1)

            def qk_scaled(r, k, n):
                dve.wait_ge(s_used[2], r)
                if isinstance(n, int) and n == 0:
                    dve.wait_ge(s_rc, 2 * k)
                V.tensor_tensor(qk_t[:, :], bank[4][:, :], r_row[:, :], ALU.mult).then_inc(s_qkc, 1)

            def transposed_lo(k, g0):
                for i in range(KT):
                    if i % 2 == 0:
                        dve.wait_ge(s_th, KT * k + i + 2)
                    src = bank[T_BANKS[k][i // 2]][:, (i % 2) * SEQ:(i % 2 + 1) * SEQ]
                    hi = t_hi[:, i, :].bitcast(fp32)
                    if g0 is None:
                        V.tensor_tensor(t_lo[:, i, :], src, hi, ALU.subtract).then_inc(s_tl, 1)
                    else:
                        V.scalar_tensor_tensor(out=t_lo[:, i, :], in0=src, scalar=g_col[:, g0 + i:g0 + i + 1], in1=hi,
                                               op0=ALU.mult, op1=ALU.subtract).then_inc(s_tl, 1)

            def ffn(f, scale):
                r0, b = R_FFN[f], f * NCH
                split_lo(0, r0[0], 2048)
                if f:
                    residual(NORM_FFN[f], scale)
                transposed_lo(T_FFN[f], f * KT)
                split_lo(1, r0[1], 2048)
                means(NORM_FFN[f])
                dve.wait_ge(s_rs, NORM_FFN[f] + 1)

                def hidden(c):
                    for t in range(NT):
                        dve.wait_ge(s_sg, (c + b) * NT + (t + 1))
                        V.scalar_tensor_tensor(out=hid[:, t, :], in0=bank[t][:, CH:2 * CH], scalar=rstd[:, t:t + 1],
                                               in1=gate[:, t, :], op0=ALU.mult, op1=ALU.mult).then_inc(s_h, 1)

                def hidden_lo(c):
                    dve.wait_ge(s_hh, c + (b + 1))
                    V.tensor_tensor(h_lo[:, :, :].rearrange("p k n -> p (k n)"), bank[2][:, :],
                                    h_hi[:, :, :].rearrange("p k n -> p (k n)").bitcast(fp32), ALU.subtract).then_inc(s_hl, 1)

                with dve.Fori(1, NCH) as c:
                    split_lo(0, c + r0[0], 2048)
                    hidden(c - 1)
                    split_lo(1, c + r0[1], 2048)
                    hidden_lo(c - 1)
                    split_lo(2, c + (r0[2] - 1), 2048)
                hidden(NCH - 1)
                split_lo(1, r0[1] + NCH, 2048)
                hidden_lo(NCH - 1)

            ffn(0, None)

            r = R_AB
            split_lo(0, r[0], 3 * LAT)
            split_lo(2, r[2], 2 * LAT)
            residual(NORM_AB, 0.5)
            transposed_lo(T_AB, 4 * KT)
            split_lo(1, r[1], 3 * LAT)
            means(NORM_AB)
            for s, (a, b) in enumerate(KS):
                split_lo(s, r[s] + 1, (b - a) * H_A * DH)
            rstd_columns(NORM_AB)
            dve.wait_ge(s_lss, 4)
            for i, n in enumerate((RQ, RKV)):
                V.tensor_scalar(lat_ms[:, :, i:i + 1], lat_ss[:, :, i:i + 1], 1.0 / n, EPS, op0=ALU.mult, op1=ALU.add).then_inc(s_lms, 1)
            dve.wait_ge(s_lrs, 1)
            dve.wait_ge(s_qb, 2)
            for t in range(NT):
                for i, (a, n) in enumerate(((0, RQ), (RQ, RKV))):
                    V.tensor_scalar(lat[:, t, a:a + n], bank[t][:, a:a + n], rstd[:, t:t + 1], lat_rstd[:, t, i:i + 1],
                                    op0=ALU.mult, op1=ALU.mult).then_inc(s_ln, 1)
            for i in range(3):
                dve.wait_ge(s_lth, (2, 2, 3)[i])
                V.scalar_tensor_tensor(out=lt_lo[:, i, :], in0=bank[2 + i // 2][:, (i % 2) * SEQ:(i % 2 + 1) * SEQ],
                                       scalar=g_col[:, G_Q + i:G_Q + i + 1], in1=lt_hi[:, i, :].bitcast(fp32),
                                       op0=ALU.mult, op1=ALU.subtract).then_inc(s_ltl, 1)
            for s, n in enumerate((H_B * QD, H_B * QD, H_B * 2 * DH)):
                split_lo(s, r[s] + 2, n)
            dve.wait_ge(s_used[2], r[2] + 3)
            for t in range(NT):
                for i in range(2):
                    dve.wait_ge(s_vb, 2 * t + i + 1)
                    V.tensor_copy(k_b[:, t, i * 4 * QD:(i + 1) * 4 * QD].rearrange("p (h d) -> p h d", d=QD)[:, :, 0:DH],
                                  bank[2 * t + i][:, :].rearrange("p (h d) -> p h d", d=2 * DH)[:, :, 0:DH]).then_inc(s_kb, 1)
            for s, (a, b) in enumerate(KS):
                split_lo(s, r[s] + 3, (b - a) * 2 * P)
            dve.wait_ge(s_qb, 2 + 4)
            dve.wait_ge(s_tab, 32)
            q9 = q_b[:, :, :].rearrange("p t (h d) -> p t h d", d=QD)
            x1, x2 = q9[:, :, :, DH:DH + 16], q9[:, :, :, DH + 16:QD]
            cos, sin = (tf(n).rearrange("p (t h d) -> p t h d", t=NT, h=9) for n in ("cos", "sin"))
            for i, (u, w) in enumerate(((x1, cos), (x2, sin), (x1, sin), (x2, cos))):
                V.tensor_tensor(rot[i][:, :, :, :], u, w, ALU.mult).then_inc(s_rt, 1)
            dve.wait_ge(s_rt, 4)
            V.tensor_tensor(x1, rot[0][:, :, :, :], rot[1][:, :, :, :], ALU.subtract).then_inc(s_ro, 1)
            V.tensor_tensor(x2, rot[2][:, :, :, :], rot[3][:, :, :, :], ALU.add).then_inc(s_ro, 1)
            dve.wait_ge(s_ro, 2)
            kr = q9[:, :, 8:9, DH:QD].to_broadcast([P, NT, H_B, ROPE])
            V.tensor_copy(k_b[:, :, :].rearrange("p t (h d) -> p t h d", d=QD)[:, :, :, DH:QD], kr).then_inc(s_kr, 1)

            qk_scaled(r[2] + 4, 1, 0)

            def maxima(n, e):
                dve.wait_ge(s_sc, 2 * n + (e + 1))
                V.tensor_reduce(nmax[:, e, 0:1], bank[e][:, 0:P], AX.X, ALU.max, negate=True)
                V.tensor_reduce(nmax[:, e, 1:2], bank[e][:, P:3 * P], AX.X, ALU.max, negate=True).then_inc(s_mx, 1)

            def outputs(n, col):
                dve.wait_ge(s_pv, n + 1)
                o = bank[7][:, 0:4 * (DH + 1)].rearrange("p (t h d) -> p t h d", t=NT, h=2)
                V.reciprocal(rden[:, :, :, :], o[:, :, :, DH:DH + 1]).then_inc(s_rd, 1)
                dve.wait_ge(s_rd, n + 1)
                V.tensor_tensor(rows[:, :, bass.ds(col, P)].rearrange("p t (h d) -> p t h d", h=2), o[:, :, :, 0:DH],
                                rden[:, :, :, :].to_broadcast([P, NT, 2, DH]), ALU.mult).then_inc(s_on, 1)

            def ab_pair(j, more):
                if more:
                    split_lo(0, j + (r[0] + 4), 3 * 2 * P)
                for e in range(2):
                    maxima(2 * j, e)
                dve.wait_ge(s_tq, 2 + j)
                V.tensor_copy(qk_b[1][0:QD, :], bank[6][0:QD, :]).then_inc(s_qbt[1], 1)
                if more:
                    split_lo(1, j + (r[1] + 4), 3 * 2 * P)
                dve.wait_ge(s_pt, 4 * j + 2)
                V.tensor_copy(pt[1][:, :], bank[3][:, 0:3 * P]).then_inc(s_pe[1], 1)
                for e in range(2):
                    maxima(2 * j + 1, e)
                if more:
                    split_lo(2, j + (r[2] + 4), 2 * 2 * P)
                outputs(2 * j, j * P)
                dve.wait_ge(s_pt, 4 * j + 4)
                V.tensor_copy(pt[1][:, :], bank[3][:, 0:3 * P]).then_inc(s_pe[1], 1)
                if more:
                    qk_scaled(j + (r[2] + 5), 1, j + 1)
                outputs(2 * j + 1, j * P + HALF)

            with dve.Fori(0, PAIRS_A - 1) as j:
                ab_pair(j, True)
            ab_pair(PAIRS_A - 1, False)
            for s, (a, b) in enumerate(KS):
                split_lo(s, r[s] + (3 + PAIRS_A), (b - a) * HALF)
            transposed_lo(T_AB_O, None)
            for s, (a, b) in enumerate(KS):
                split_lo(s, r[s] + (4 + PAIRS_A), (b - a) * HALF)

            ffn(1, 1.0)
            ffn(2, 0.5)

            r = R_C
            split_lo(0, r[0], 3 * HALF)
            split_lo(2, r[2], 2 * HALF)
            residual(NORM_C, 0.5)
            transposed_lo(T_C, 5 * KT)
            split_lo(1, r[1], 3 * HALF)
            means(NORM_C)
            for s, (a, b) in enumerate(KS):
                split_lo(s, r[s] + 1, (b - a) * HALF)
            rstd_columns(NORM_C)
            for s, (a, b) in enumerate(KS):
                split_lo(s, r[s] + 2, (b - a) * 2 * P)
            qk_scaled(r[2] + 3, 2, 0)

            def c_pair(j, more):
                if more:
                    for s, (a, b) in enumerate(KS[:2]):
                        split_lo(s, j + (r[s] + 3), (b - a) * 2 * P)
                for e in range(2):
                    dve.wait_ge(s_zl, 2 * j + (e + 1))
                    V.scalar_tensor_tensor(out=sp[e][:, :], in0=bank[e][:, 0:3 * P], scalar=0.0, in1=sp_abs[e][:, :],
                                           op0=ALU.max, op1=ALU.add).then_inc(s_sp, 1)
                if more:
                    split_lo(2, j + (r[2] + 3), 2 * 2 * P)
                    qk_scaled(j + (r[2] + 4), 2, j + 1)

            with dve.Fori(0, PAIRS_C - 1) as j:
                c_pair(j, True)
            c_pair(PAIRS_C - 1, False)
            for s, (a, b) in enumerate(KS):
                split_lo(s, r[s] + (2 + PAIRS_C), (b - a) * HALF)
            transposed_lo(T_C_O, None)
            for s, (a, b) in enumerate(KS):
                split_lo(s, r[s] + (3 + PAIRS_C), (b - a) * HALF)
            ffn(3, 1.0)

            residual(NORM_END, 0.5)
            means(NORM_END)
            dve.wait_ge(s_gf, 16)
            dve.wait_ge(s_rs, NORM_END + 1)
            for t in range(NT):
                V.scalar_tensor_tensor(out=rows[:, t, :], in0=xres[:, t, :], scalar=rstd[:, t:t + 1], in1=g_fin[:, :],
                                       op0=ALU.mult, op1=ALU.mult).then_inc(s_y, 1)

        @block.tensor
        def _(pe):
            MM = nc.tensor.matmul
            pe.sem_inc(s_tq, 1)
            pe.sem_inc(s_on, 1)
            pe.sem_inc(s_oe, 1)

            def mm3(dst, a_hi, a_lo, b_hi, b_lo, start, stop):
                MM(dst, a_hi, b_hi, start=start, stop=False)
                MM(dst, a_hi, b_lo, start=False, stop=False)
                return MM(dst, a_lo, b_hi, start=False, stop=stop)

            def transposes(k, src, ready):
                for t in range(NT):
                    for h in range(2):
                        ready(t, h)
                        for i in range(h * KT // 2, (h + 1) * KT // 2):
                            at = (i % 2) * SEQ + t * P
                            end = nc.tensor.transpose(bank[T_BANKS[k][i // 2]][:, at:at + P], src[:, t, i * P:(i + 1) * P], ident)
                        if t == NT - 1:
                            end.then_inc(s_xt, 1)

            def residual_ready(n):
                def ready(t, h):
                    if n:
                        pe.wait_ge(s_x, 4 * (n - 1) + 2 * t + h + 1)
                    elif h == 0:
                        pe.wait_ge(s_in[t], 16)
                return ready

            def rstd_transposed(k):
                pe.wait_ge(s_rb, k)
                for t in range(NT):
                    end = MM(bank[7][:, t * P:(t + 1) * P], r_sq[:, t, :], ident, start=t == 0, stop=t == 1,
                             skip_group_check=True)
                end.then_inc(s_rr, 1)

            T = (t_hi, t_lo)

            def by_slot(slot, r, tiles, lhs, n, dst, first, last, tile_done=None):
                pe.wait_ge(s_lo[slot], r + 1)
                for t in range(NT):
                    outs = dst(t)
                    for i, k in enumerate(tiles):
                        hi, lo = (x[:, k, t * P:(t + 1) * P] for x in lhs)
                        for m, o in enumerate(outs):
                            c = (i * len(outs) + m) * n
                            end = mm3(o, hi, lo, w_hi[slot][:, c:c + n], w_lo[slot][:, c:c + n],
                                      first and i == 0, last and i == len(tiles) - 1)
                    if t == 0 and tile_done is not None:
                        end.then_inc(tile_done, 1)
                end.then_inc(s_used[slot], 1)

            def block_round(R, r, n, dst, tile_done=None, k=None):
                for s, (a, b) in enumerate(KS):
                    if k is not None:
                        pe.wait_ge(s_tl, KT * k + b)
                    by_slot(s, R[s] + r, range(a, b), T, n, dst, s == 0, s == 2, tile_done if s == 2 else None)

            def ffn(f):
                r0, b = R_FFN[f], f * NCH
                n = NORM_FFN[f]
                transposes(T_FFN[f], xres, residual_ready(n))

                def up(c, slot):
                    by_slot(slot, c + r0[slot], range(4 * slot, 4 * slot + 4), T, 2 * CH, lambda t: [bank[t][:, :]],
                            slot == 0, slot == 1, s_gu if slot == 1 else None)

                def turn(c):
                    for t in range(NT):
                        pe.wait_ge(s_h, (c + b) * NT + (t + 1))
                        for k in range(FT):
                            end = nc.tensor.transpose(bank[2][:, k * SEQ + t * P:k * SEQ + (t + 1) * P],
                                                      hid[:, t, k * P:(k + 1) * P], ident)
                    end.then_inc(s_ht, 1)

                def down(c, slot, r, first, last):
                    pe.wait_ge(s_hl, c + (b + 1))
                    by_slot(slot, c + r, range(FT), (h_hi, h_lo), HALF, lambda t: [acc[t][h][:, :] for h in range(2)],
                            first, last, s_acc if last else None)

                for s in range(2):
                    pe.wait_ge(s_tl, KT * T_FFN[f] + 4 * s + 4)
                    up(0, s)
                turn(0)
                up(1, 0)
                up(1, 1)
                down(0, 2, r0[2], True, False)
                with pe.Fori(2, NCH) as c:
                    turn(c - 1)
                    up(c, 0)
                    up(c, 1)
                    down(c - 1, 2, r0[2], False, False)
                turn(NCH - 1)
                down(NCH - 1, 1, r0[1] + 1, False, True)

            pe.wait_ge(s_id, 16)
            pe.wait_ge(s_gr, 4 * 16)
            nc.tensor.transpose(bank[7][:, 0:N_G], g_rows[0:N_G, :], ident[0:N_G, 0:N_G]).then_inc(s_gt, 1)
            ffn(0)

            r = R_AB
            transposes(T_AB, xres, residual_ready(NORM_AB))
            block_round(r, 0, LAT, lambda t: [bank[t][:, 0:LAT]], k=T_AB)
            block_round(r, 1, H_A * DH, lambda t: [bank[4 + t][:, :]])
            rstd_transposed(1)
            pe.wait_ge(s_ln, 4)
            for t in range(NT):
                for i in range(3):
                    end = nc.tensor.transpose(bank[2 + i // 2][:, (i % 2) * SEQ + t * P:(i % 2) * SEQ + (t + 1) * P],
                                              lat[:, t, i * P:(i + 1) * P], ident)
            end.then_inc(s_lt, 1)
            pe.wait_ge(s_ltl, 3)
            pe.wait_ge(s_vc, NT)
            LT = (lt_hi, lt_lo)
            q_banks = lambda t: [bank[(6, 4)[t] + i][:, 0:4 * QD] for i in range(2)]
            by_slot(0, r[0] + 2, [0], LT, 4 * QD, q_banks, True, False)
            by_slot(1, r[1] + 2, [1], LT, 4 * QD, q_banks, False, True)
            by_slot(2, r[2] + 2, [2], LT, 4 * 2 * DH, lambda t: [bank[2 * t + i][:, :] for i in range(2)], True, True)

            def project_qk(slot, r, bk):
                a, b = KS[slot]
                pe.wait_ge(s_lo[slot], r + 1)
                for k in range(a, b):
                    for i in range(2):
                        c = ((k - a) * 2 + i) * P
                        dst = bk[:, i * SEQ:(i + 1) * SEQ]
                        hi, lo = w_hi[slot][:, c:c + P], w_lo[slot][:, c:c + P]
                        MM(dst, hi, t_hi[:, k, :], start=k == 0 and i == 0, stop=False, skip_group_check=True)
                        MM(dst, hi, t_lo[:, k, :], start=False, stop=False, skip_group_check=True)
                        end = MM(dst, lo, t_hi[:, k, :], start=False, stop=k == KT - 1 and i == 1, skip_group_check=True)
                end.then_inc(s_used[slot], 1)

            pe.wait_ge(s_qb, 2 + 4)
            for s in range(3):
                project_qk(s, r[s] + 3, bank[4])
            pe.wait_ge(s_kb, 4)
            pe.wait_ge(s_vb, 4)

            def scores_a(j):
                pe.wait_ge(s_qkc, j + 1)
                for e in range(2):
                    q, k = (qk_t[e * DH:(e + 1) * DH, i * SEQ:(i + 1) * SEQ] for i in range(2))
                    MM(bank[e][:, 0:3 * P], tabb[:, bass.ds(j * (2 * P) + (BC["slopes"][0] + e * P), P)], tb("dist"), start=True, stop=False, skip_group_check=True)
                    MM(bank[e][:, 0:P], q[:, 0:P], k[:, 0:P], start=False, stop=False, skip_group_check=True)
                    MM(bank[e][:, P:3 * P], q[:, P:SEQ], k, start=False, stop=True, skip_group_check=True).then_inc(s_sc, 1)

            def scores_b():
                for e in range(2):
                    q, k = (qk_b[e][0:QD, i * SEQ:(i + 1) * SEQ] for i in range(2))
                    MM(bank[e][:, 0:3 * P], tb("identb"), tb("causal"), start=True, stop=False, skip_group_check=True)
                    MM(bank[e][:, 0:P], q[:, 0:P], k[:, 0:P], start=False, stop=False, skip_group_check=True)
                    MM(bank[e][:, P:3 * P], q[:, P:SEQ], k, start=False, stop=True, skip_group_check=True).then_inc(s_sc, 1)

            def turn_probs(src, e):
                for i in range(3):
                    end = nc.tensor.transpose(bank[2 + e][:, i * P:(i + 1) * P], src[e][:, i * P:(i + 1) * P], ident)
                end.then_inc(s_pt, 1)

            def weigh(n, v, col):
                pe.wait_ge(s_pe[0], n + 1)
                pe.wait_ge(s_pe[1], n + 1)
                pe.wait_ge(s_on, n + 1)
                for t in range(NT):
                    for e in range(2):
                        w = DH + 1
                        dst = bank[7][:, (2 * t + e) * w:(2 * t + e + 1) * w]
                        for i in range(t + 1):
                            end = MM(dst, pt[e][:, (t + i) * P:(t + i + 1) * P], v[:, i, bass.ds(col + e * w, w)],
                                     start=t == 0 and e == 0, stop=t == 1 and e == 1 and i == 1, skip_group_check=True)
                end.then_inc(s_pv, 1)

            def ab_pair(j, more):
                scores_a(j)
                pe.wait_ge(s_st, 2 * j + 2)
                for e in range(2):
                    for i, st in enumerate((q_st, k_st)):
                        for t in range(NT):
                            end = nc.tensor.transpose(bank[5 + e][0:QD, i * SEQ + t * P:i * SEQ + (t + 1) * P],
                                                      st[:, t, e * QD:(e + 1) * QD], ident)
                end.then_inc(s_tq, 1)
                if more:
                    project_qk(0, j + (r[0] + 4), bank[4])
                for e in range(2):
                    pe.wait_ge(s_cn, 2 * j + (e + 1))
                    turn_probs(pc, e)
                for e in range(2):
                    pe.wait_ge(s_qbt[e], j + 1)
                scores_b()
                if more:
                    project_qk(1, j + (r[1] + 4), bank[4])
                weigh(2 * j, v_a, j * (2 * (DH + 1)))
                for e in range(2):
                    pe.wait_ge(s_ex, 4 * j + (e + 3))
                    turn_probs(pr, e)
                if more:
                    project_qk(2, j + (r[2] + 4), bank[4])
                weigh(2 * j + 1, v_b, j * (2 * (DH + 1)))

            with pe.Fori(0, PAIRS_A - 1) as j:
                ab_pair(j, True)
            ab_pair(PAIRS_A - 1, False)

            def project_out(R, r, k):
                block_round(R, r, HALF, lambda t: [acc[t][0][:, :]], k=k)
                block_round(R, r + 1, HALF, lambda t: [acc[t][1][:, :]], s_acc)

            transposes(T_AB_O, rows, lambda t, h: pe.wait_ge(s_on, 1 + 2 * PAIRS_A))
            project_out(R_AB, 3 + PAIRS_A, T_AB_O)
            ffn(1)
            ffn(2)

            r = R_C
            transposes(T_C, xres, residual_ready(NORM_C))
            block_round(r, 0, HALF, lambda t: [bank[t][:, :]], k=T_C)
            block_round(r, 1, HALF, lambda t: [bank[2 + t][:, :]])
            rstd_transposed(2)
            for s in range(3):
                project_qk(s, r[s] + 2, bank[4])
            pe.wait_ge(s_vc, 3 * NT)

            def c_pair(j, more):
                pe.wait_ge(s_qkc, j + (PAIRS_A + 1))
                for e in range(2):
                    q, k = (qk_t[e * DH:(e + 1) * DH, i * SEQ:(i + 1) * SEQ] for i in range(2))
                    MM(bank[e][:, 0:3 * P], tb("identb"), tb("strict"), start=True, stop=False, skip_group_check=True)
                    MM(bank[e][:, 0:SEQ], k[:, 0:P], q, start=False, stop=False, skip_group_check=True)
                    MM(bank[e][:, SEQ:3 * P], k[:, P:SEQ], q[:, P:SEQ], start=False, stop=True,
                       skip_group_check=True).then_inc(s_z, 1)
                if more:
                    project_qk(0, j + (r[0] + 3), bank[4])
                    project_qk(1, j + (r[1] + 3), bank[4])
                for e in range(2):
                    pe.wait_ge(s_sp, 2 * j + (e + 1))
                    MM(bank[e][:, 0:3 * P], tf("neg_tri"), sp[e][:, :], start=False, stop=False, skip_group_check=True)
                    MM(bank[e][:, P:SEQ], tf("neg_one"), sp[e][:, SEQ:], start=False, stop=True,
                       skip_group_check=True).then_inc(s_cs, 1)
                if more:
                    project_qk(2, j + (r[2] + 3), bank[4])
                pe.wait_ge(s_oe, j + 1)
                for e in range(2):
                    pe.wait_ge(s_at, 2 * j + (e + 1))
                    for t in range(NT):
                        dst = bank[3][:, (2 * t + e) * DH:(2 * t + e + 1) * DH]
                        for i in range(t + 1):
                            c = (t + i) * P
                            end = MM(dst, pr[e][:, c:c + P], v_c[:, i, bass.ds(j * P + e * DH, DH)],
                                     start=t == 0 and e == 0, stop=e == 1 and t == 1 and i == 1, skip_group_check=True)
                end.then_inc(s_oc, 1)

            with pe.Fori(0, PAIRS_C - 1) as j:
                c_pair(j, True)
            c_pair(PAIRS_C - 1, False)
            transposes(T_C_O, rows, lambda t, h: pe.wait_ge(s_oe, 1 + PAIRS_C))
            project_out(R_C, 2 + PAIRS_C, T_C_O)
            ffn(3)


_INS = ["x", "ffn_norm_g", "mix_norm_g", "ffn_w_gate", "ffn_w_up", "ffn_w_down", "ab_w_in", "mla_q_norm_g",
        "mla_w_uq", "mla_kv_norm_g", "mla_w_ukv", "ab_w_out", "sb_w_in", "sb_w_out", "final_norm_g"]


def tables(np):
    f, nf, b, nb = layout(1024, 2816, 256)
    tf, tb = np.zeros((P, nf), np.float32), np.zeros((P, nb), np.float32)
    row, col = np.arange(P)[:, None], np.arange(P)[None, :]

    def put(t, at, name, values):
        t[:, at[name][0]:at[name][1]] = np.asarray(values, np.float32).reshape(P, -1)

    put(tf, f, "ident", row == col)
    put(tf, f, "neg_tri", -1.0 * (row >= col))
    put(tf, f, "neg_one", -np.ones((P, P)))
    dist = np.concatenate([row - col, row - col + P, row - col], axis=1)
    count = (dist >= 0) * ((dist <= 128) * 1 + (dist % 4 == 0) + (dist % 16 == 0))
    put(tf, f, "count", count)
    put(tb, b, "dist", np.where(count > 0, -dist, NEG))
    put(tb, b, "causal", np.where(dist >= 0, 0.0, NEG))
    put(tb, b, "identb", row == col)
    put(tb, b, "slopes", np.concatenate([2.0 ** -(h + 1) * (row == col) for h in range(8)], axis=1))
    strict = np.where(row < col, 0.0, NEG)
    put(tb, b, "strict", np.concatenate([strict, np.zeros((P, P)), strict], axis=1))
    inv = np.float32(10000.0) ** (-np.arange(0, 32, 2, dtype=np.float32) / np.float32(32))
    ang = np.arange(256, dtype=np.float32)[:, None] * inv[None, :].astype(np.float32)
    for name, fn in (("cos", np.cos), ("sin", np.sin)):
        put(tf, f, name, np.repeat(fn(ang).reshape(2, P, 1, 16).transpose(1, 0, 2, 3), 9, axis=2))
    return tf, (tb.view(np.uint32) >> 16).astype(np.uint16)


def kernel(**inputs):
    import numpy as np
    import concourse.bacc as bacc
    from concourse.bass_utils import run_bass_kernel_spmd

    nc = bacc.Bacc("TRN2", target_bir_lowering=False, num_devices=1)
    arrays, args = {}, []
    table_f, table_b = tables(np)
    for name, a in [(n, inputs[n]) for n in _INS] + [("table_f", table_f), ("table_b", table_b)]:
        a = np.ascontiguousarray(a)
        arrays[f"in_{name}_dram"] = a
        args.append(nc.dram_tensor(f"in_{name}_dram", a.shape, mybir.dt.from_np(a.dtype), kind="ExternalInput").ap())
    shape = tuple(inputs["x"].shape)
    out = nc.dram_tensor("out_0_dram", shape, mybir.dt.float32, kind="ExternalOutput").ap()
    trunk_kernel(nc, *args, out)
    r = run_bass_kernel_spmd(nc, [arrays], core_ids=[0])
    return r.results[0]["out_0_dram"]
```

```python
import concourse.bass as bass
from concourse import mybir
from contextlib import ExitStack


P = 128
NEG = -1e30


def layout(D, F, SEQ):
    f, b, at_f, at_b = {}, {}, 0, 0
    for name, n in (("ident", P), ("neg_tri", P), ("neg_one", P), ("count", 3 * P),
                    ("cos", 2 * 9 * 16), ("sin", 2 * 9 * 16)):
        f[name] = (at_f, at_f + n)
        at_f += n
    for name, n in (("identb", P), ("slopes", 8 * P), ("dist", 3 * P), ("causal", 3 * P), ("strict", 3 * P)):
        b[name] = (at_b, at_b + n)
        at_b += n
    return f, at_f, b, at_b


def trunk_kernel(nc, x, ffn_norm_g, mix_norm_g, w_gate, w_up, w_down, ab_w_in, q_norm_g, w_uq, kv_norm_g,
                 w_ukv, ab_w_out, sb_w_in, sb_w_out, final_norm_g, table_f, table_b, out):
    fp32, f32r, bf16, u16 = mybir.dt.float32, mybir.dt.float32r, mybir.dt.bfloat16, mybir.dt.uint16
    ALU, ACT, AX = mybir.AluOpType, mybir.ActivationFunctionType, mybir.AxisListType

    _, SEQ, D = x.shape
    F = w_gate.shape[-1]
    EPS = 1e-6
    NT = SEQ // P
    KT = D // P
    HALF = D // 2
    CH = 256
    NCH = F // CH
    FT = CH // P
    KS = ((0, 3), (3, 6), (6, 8))
    DH = 64
    H_A, H_B, H_C = 8, 8, 16
    QD, ROPE = 96, 32
    RQ, RKV = q_norm_g.shape[-1], kv_norm_g.shape[-1]
    LAT = RQ + RKV + ROPE
    A_QKV = 3 * H_A * DH
    PAIRS_A, PAIRS_C = H_A // 2, H_C // 2
    G_Q = 6 * KT
    G_KV = G_Q + RQ // P
    N_G = G_KV + RKV // P

    ctx = ExitStack()
    with ctx:
        def sb(name, shape, dt=fp32):
            return ctx.enter_context(nc.sbuf_tensor(name, shape, dt))

        def sem(name):
            return ctx.enter_context(nc.semaphore(name))

        raw = [sb(f"raw{s}", [P, 2048]) for s in range(3)]
        w_hi = [sb(f"w_hi{s}", [P, 2048], f32r) for s in range(3)]
        w_lo = [sb(f"w_lo{s}", [P, 2048], f32r) for s in range(3)]
        xres = sb("xres", [P, NT, D])
        rows = sb("rows", [P, NT, D])
        t_hi = sb("t_hi", [P, KT, SEQ], f32r)
        t_lo = sb("t_lo", [P, KT, SEQ], f32r)
        junk = sb("junk", [P, D])
        hid = sb("hid", [P, NT, CH])
        gate = sb("gate", [P, NT, CH])
        h_hi = sb("h_hi", [P, FT, SEQ], f32r)
        h_lo = sb("h_lo", [P, FT, SEQ], f32r)
        ss_h = sb("ss_h", [P, NT, 2])
        m_0 = sb("m_0", [P, NT])
        ss = sb("ss", [P, NT])
        ms = sb("ms", [P, NT])
        rstd = sb("rstd", [P, NT])
        r_sq = sb("r_sq", [P, NT, P])
        r_row = sb("r_row", [P, 2 * SEQ])
        half_neg = sb("half_neg", [P, 4])
        g_rows = sb("g_rows", [P, P])
        g_col = sb("g_col", [P, P])
        g_fin = sb("g_fin", [P, D])
        FC, nf, BC, nb = layout(D, F, SEQ)
        tabf = sb("tabf", [P, nf])
        tabb = sb("tabb", [P, nb], bf16)
        qk_t = sb("qk_t", [P, 2 * SEQ])
        pr = [sb(f"pr{e}", [P, 3 * P]) for e in range(2)]
        pc = [sb(f"pc{e}", [P, 3 * P]) for e in range(2)]
        pt = [sb(f"pt{e}", [P, 3 * P]) for e in range(2)]
        nmax = sb("nmax", [P, 2, NT])
        rden = sb("rden", [P, NT, 2, 1])
        v_a = sb("v_a", [P, NT, H_A * (DH + 1)])
        v_b = sb("v_b", [P, NT, H_B * (DH + 1)])
        v_c = sb("v_c", [P, NT, H_C * DH])
        lat = sb("lat", [P, NT, RQ + RKV])
        lat_ss = sb("lat_ss", [P, NT, 2])
        lat_ms = sb("lat_ms", [P, NT, 2])
        lat_rstd = sb("lat_rstd", [P, NT, 2])
        lt_hi = sb("lt_hi", [P, 3, SEQ], f32r)
        lt_lo = sb("lt_lo", [P, 3, SEQ], f32r)
        q_b = sb("q_b", [P, NT, 9 * QD])
        k_b = sb("k_b", [P, NT, H_B * QD])
        rot = [sb(f"rot{i}", [P, NT, 9, 16]) for i in range(4)]
        q_st = sb("q_st", [P, NT, 2 * QD])
        k_st = sb("k_st", [P, NT, 2 * QD])
        qk_b = [sb(f"qk_b{e}", [P, 2 * SEQ]) for e in range(2)]
        W = 3 * P
        sp_abs, sp_log = ([q_b[:, e, i * W:(i + 1) * W] for e in range(2)] for i in range(2))
        sp_exp, sp = ([k_b[:, e, i * W:(i + 1) * W] for e in range(2)] for i in range(2))
        sp_hi = [sb(f"sp_hi{e}", [P, 3 * P], f32r) for e in range(2)]
        sp_lo = [sb(f"sp_lo{e}", [P, 3 * P], f32r) for e in range(2)]
        tri_r = sb("tri_r", [P, P], f32r)
        one_r = sb("one_r", [P, P], f32r)

        bank = [ctx.enter_context(nc.psum_tensor(f"bank{i}", [P, 512], fp32)) for i in range(8)]
        acc = [[bank[4 + 2 * t + h] for h in range(2)] for t in range(NT)]

        def tf(name):
            return tabf[:, FC[name][0]:FC[name][1]]

        def tb(name, lo=0, hi=None):
            a, b = BC[name]
            return tabb[:, a + lo:(b if hi is None else a + hi)]

        ident = tf("ident")

        s_in = [sem(f"x_loaded{t}") for t in range(NT)]
        s_id = sem("identity_loaded")
        s_tab = sem("tables_loaded")
        s_gr = sem("gain_rows_loaded")
        s_gf = sem("final_gain_loaded")
        s_raw = [sem(f"raw_loaded{s}") for s in range(3)]
        s_hi = [sem(f"high_ready{s}") for s in range(3)]
        s_lo = [sem(f"low_ready{s}") for s in range(3)]
        s_used = [sem(f"weights_used{s}") for s in range(3)]
        s_half = sem("constants_set")
        s_gt = sem("gains_transposed")
        s_gc = sem("gains_ready")
        s_acc = sem("sublayer_summed")
        s_x = sem("residual_updated")
        s_ss = sem("squares_summed")
        s_ms = sem("mean_square_ready")
        s_rs = sem("rstd_ready")
        s_rb = sem("rstd_repeated")
        s_rr = sem("rstd_transposed")
        s_rc = sem("rstd_rows_ready")
        s_xt = sem("rows_transposed")
        s_th = sem("transpose_high_ready")
        s_tl = sem("transpose_low_ready")
        s_gu = sem("gate_up_summed")
        s_sg = sem("silu_ready")
        s_h = sem("hidden_ready")
        s_ht = sem("hidden_transposed")
        s_hh = sem("hidden_high_ready")
        s_hl = sem("hidden_low_ready")
        s_vc = sem("v_copied")
        s_qkc = sem("qk_copied")
        s_lss = sem("latent_squares_summed")
        s_lms = sem("latent_mean_square_ready")
        s_lrs = sem("latent_rstd_ready")
        s_ln = sem("latents_normed")
        s_lt = sem("latents_transposed")
        s_lth = sem("latent_high_ready")
        s_ltl = sem("latent_low_ready")
        s_qb = sem("mla_q_copied")
        s_kb = sem("mla_k_copied")
        s_vb = sem("mla_v_copied")
        s_rt = sem("rotary_products_ready")
        s_ro = sem("rotary_applied")
        s_kr = sem("mla_k_complete")
        s_st = sem("mla_pair_staged")
        s_tq = sem("mla_pair_transposed")
        s_qbt = [sem(f"mla_head_ready{e}") for e in range(2)]
        s_sc = sem("scores_ready")
        s_mx = sem("max_ready")
        s_ex = sem("exp_ready")
        s_cn = sem("counted")
        s_pt = sem("probs_transposed")
        s_pe = [sem(f"probs_copied{e}") for e in range(2)]
        s_pv = sem("pv_summed")
        s_rd = sem("denominators_inverted")
        s_on = sem("outputs_normed")
        s_z = sem("z_ready")
        s_za = sem("z_magnitude")
        s_sh = sem("softplus_high_ready")
        s_sl = sem("softplus_low_ready")
        s_tri = sem("triangles_ready")
        s_ze = sem("z_exp_ready")
        s_zl = sem("z_log_ready")
        s_sp = sem("softplus_ready")
        s_cs = sem("logits_ready")
        s_at = sem("weights_ready")
        s_oc = sem("stick_summed")
        s_oe = sem("stick_copied")
        s_m0 = sem("half_mean_ready")
        s_xg = sem("gained_rows_ready")
        s_y0 = sem("final_half_0_ready")
        s_y1 = sem("final_half_1_ready")
        s_out = sem("stored")

        block = ctx.enter_context(nc.Block())

        FFN_ROUNDS = (NCH, NCH + 1, NCH - 1)
        A_ROUNDS, C_ROUNDS = (3 + PAIRS_A + 2,) * 3, (2 + PAIRS_C + 2,) * 3
        R_NORM = [(0, 0, 0)]
        for rounds in (FFN_ROUNDS, A_ROUNDS, FFN_ROUNDS, FFN_ROUNDS, C_ROUNDS, FFN_ROUNDS):
            R_NORM.append(tuple(a + b for a, b in zip(R_NORM[-1], rounds)))
        NORM_FFN, NORM_AB, NORM_C, NORM_END = [0, 2, 3, 5], 1, 4, 6
        R_FFN, R_AB, R_C = [R_NORM[n] for n in NORM_FFN], R_NORM[NORM_AB], R_NORM[NORM_C]
        PARTS = lambda n: [(0, 0), (1, 0), (0, 1), (1, 1)] if n == NORM_END else [(0, 0), (0, 1), (1, 0), (1, 1)]
        ACC_NORM = [0]
        for n in range(NORM_END):
            ACC_NORM.append(ACC_NORM[-1] + (3 if n in NORM_FFN else 2))
        WARM_UP = 4
        UP_BANKS = lambda c: (6, 7) if isinstance(c, int) and c == 0 else (0, 1)
        T_FFN, T_AB, T_AB_O, T_C, T_C_O = [0, 3, 4, 7], 1, 2, 5, 6
        T_NORM = [0, 1, 3, 4, 5, 7]
        T_BANKS = {k: (2, 3, 4, 5) for k in range(8)}
        T_BANKS[T_AB_O], T_BANKS[T_C_O] = (4, 5, 0, 1), (7, 0, 1, 2)
        T_ORDER = {k: list(range(KT)) for k in range(8)}
        T_ORDER[T_AB_O] = [i for i in range(KT) if i % PAIRS_A < PAIRS_A - 1] + [PAIRS_A - 1, KT - 1]
        Z_BANKS = ((0, 1), (2, 3))

        @block.sync
        def _(sp_):
            def load(slot, r, parts):
                if not (isinstance(r, int) and r == 0):
                    sp_.wait_ge(s_lo[slot], r)
                for dst, src in parts:
                    sp_.dma_start(dst, src).then_inc(s_raw[slot], 16)

            def load_up(f, c, slot):
                kt = slice(4 * slot, 4 * slot + 4)
                dst = raw[slot][:, :].rearrange("p (k b n) -> p k b n", k=4, b=2)
                load(slot, c + R_FFN[f][slot], [
                    (dst[:, :, b, :], w[f // 2, f % 2].rearrange("(k p) n -> p k n", p=P)[:, kt, bass.ds(c * CH, CH)])
                    for b, w in ((0, w_gate), (1, w_up))])

            def load_down(f, c, slot, r):
                src = w_down[f // 2, f % 2]
                load(slot, c + r, [
                    (raw[slot][:, i * D:(i + 1) * D], src[bass.ds(c * CH + i * P, P), :]) for i in range(FT)])

            def load_ffn(f):
                if f:
                    for s in range(2):
                        load_up(f, 0, s)
                with sp_.Fori(1, NCH) as c:
                    for s in range(2):
                        load_up(f, c, s)
                    load_down(f, c - 1, 2, R_FFN[f][2])
                load_down(f, NCH - 1, 1, R_FFN[f][1] + 1)

            def load_block(w, R, r, col, n):
                src = w.rearrange("(k p) n -> p k n", p=P)
                for s, (a, b) in enumerate(KS):
                    dst = raw[s][:, 0:(b - a) * n].rearrange("p (k n) -> p k n", k=b - a)
                    load(s, R[s] + r, [(dst[:, 0:1, :], src[:, a:a + 1, bass.ds(col, n)]),
                                (dst[:, 1:, :], src[:, a + 1:b, bass.ds(col, n)])])

            def load_qk(w, R, r, j, width):
                src = w.rearrange("(k p) n -> p k n", p=P)
                for s, (a, b) in enumerate(KS):
                    dst = raw[s][:, 0:(b - a) * 2 * P].rearrange("p (k b n) -> p k b n", k=b - a, b=2)
                    load(s, R[s] + r, [(dst[:, :, i, :], src[:, a:b, bass.ds(j * P + i * width, P)]) for i in range(2)])

            sp_.dma_start(tabf[:, 0:P], table_f[:, 0:P]).then_inc(s_id, 16)
            load_up(0, 0, 0)
            for t in range(NT):
                sp_.dma_start(xres[:, t, :], x[0, t * P:(t + 1) * P, :]).then_inc(s_in[t], 16)
            load_up(0, 0, 1)

            load_ffn(0)
            sp_.dma_start(tabb[:, :].bitcast(u16), table_b).then_inc(s_tab, 16)
            sp_.dma_start(tabf[:, P:], table_f[:, P:]).then_inc(s_tab, 16)
            sp_.dma_start(g_fin[:, :], final_norm_g.partition_broadcast(P)).then_inc(s_gf, 16)
            load_block(ab_w_in[0], R_AB, 0, A_QKV, LAT)
            load_block(ab_w_in[0], R_AB, 1, 2 * H_A * DH, H_A * DH)
            load_qk(ab_w_in[0], R_AB, 2, 0, H_A * DH)
            for s in range(RQ // P):
                n = H_B * QD // 2
                load(s, R_AB[s] + 3, [(raw[s][:, i * n:(i + 1) * n], w_uq[0, s * P:(s + 1) * P, i * n:(i + 1) * n])
                                      for i in range(2)])
            n = H_B * 2 * DH // 2
            load(2, R_AB[2] + 3, [(raw[2][:, i * n:(i + 1) * n], w_ukv[0, :, i * n:(i + 1) * n]) for i in range(2)])
            with sp_.Fori(1, PAIRS_A) as j:
                load_qk(ab_w_in[0], R_AB, 3 + j, j, H_A * DH)
            with sp_.Fori(0, 2) as j:
                load_block(ab_w_out[0], R_AB, 3 + PAIRS_A + j, j * HALF, HALF)
            load_ffn(1)
            load_ffn(2)
            with sp_.Fori(0, 2) as j:
                load_block(sb_w_in[0], R_C, j, 2 * D + j * HALF, HALF)
            with sp_.Fori(0, PAIRS_C) as j:
                load_qk(sb_w_in[0], R_C, 2 + j, j, D)
            with sp_.Fori(0, 2) as j:
                load_block(sb_w_out[0], R_C, 2 + PAIRS_C + j, j * HALF, HALF)
            load_ffn(3)
            for t in range(NT):
                for h, done in enumerate((s_y0, s_y1)):
                    cols = slice(h * HALF, (h + 1) * HALF)
                    sp_.wait_ge(done, t + 1)
                    sp_.dma_start(out[0, t * P:(t + 1) * P, cols], xres[:, t, cols]).then_inc(s_out, 16)
            sp_.wait_ge(s_out, 16 * NT * 2)

        @block.gpsimd
        def _(pool):
            nc.gpsimd.memset(half_neg[:, :], -0.5).then_inc(s_half, 1)
            nc.gpsimd.memset(v_a[:, :, :], 1.0).then_inc(s_half, 1)
            nc.gpsimd.memset(v_b[:, :, :], 1.0).then_inc(s_half, 1)
            pool.wait_ge(s_half, 3)

            def root(n):
                pool.wait_ge(s_ms, n + 1)
                nc.gpsimd.tensor_tensor(rstd[:, :], ms[:, :], half_neg[:, 0:NT], ALU.pow).then_inc(s_rs, 1)

            root(NORM_FFN[0])
            root(NORM_AB)
            pool.wait_ge(s_lms, 2)
            nc.gpsimd.tensor_tensor(lat_rstd[:, :, :].rearrange("p t n -> p (t n)"),
                                    lat_ms[:, :, :].rearrange("p t n -> p (t n)"), half_neg[:, :], ALU.pow).then_inc(s_lrs, 1)
            pool.wait_ge(s_tab, 32)
            pool.wait_ge(s_ro, 2)
            pool.wait_ge(s_kr, 1)

            def counted(j):
                for e in range(2):
                    pool.wait_ge(s_ex, j * 4 + (e + 1))
                    nc.gpsimd.tensor_tensor(pc[e][:, :], pr[e][:, :], tf("count"), ALU.mult).then_inc(s_cn, 1)

            with pool.Fori(0, PAIRS_A - 1) as j:
                counted(j)
                pool.wait_ge(s_tq, j + 1)
                at = bass.ds(j * (2 * QD) + 2 * QD, 2 * QD)
                nc.gpsimd.tensor_copy(q_st[:, :, :], q_b[:, :, at]).then_inc(s_st, 1)
                nc.gpsimd.tensor_copy(k_st[:, :, :], k_b[:, :, at]).then_inc(s_st, 1)
            counted(PAIRS_A - 1)
            for n in range(2, NORM_END):
                root(n)
            for t in range(NT):
                pool.wait_ge(s_ms, NORM_END + t + 1)
                nc.gpsimd.tensor_tensor(rstd[:, t:t + 1], ms[:, t:t + 1], half_neg[:, 0:1], ALU.pow).then_inc(s_rs, 1)

        @block.scalar
        def _(act):
            A = nc.scalar.activation

            def split_hi(slot, r, n):
                act.wait_ge(s_raw[slot], r * 32 + 32)
                if not (isinstance(r, int) and r == 0):
                    act.wait_ge(s_used[slot], r)
                A(w_hi[slot][:, 0:n], raw[slot][:, 0:n], ACT.Copy).then_inc(s_hi[slot], 1)

            def squares(n):
                for t in range(NT):
                    if n == 0:
                        act.wait_ge(s_in[t], 16)
                    else:
                        act.wait_ge(s_x, 4 * (n - 1) + 3 + t)
                    if NT * n + t:
                        act.wait_ge(s_ss, NT * n + t)
                    if n == NORM_AB + 1:
                        act.wait_ge(s_lss, 4)
                    A(junk[:, :], xres[:, t, :], ACT.Square, accum_out=ss[:, t:t + 1]).then_inc(s_ss, 1)

            def transposed_hi(k, g0, tiles=range(KT)):
                for i in tiles:
                    if i % 2 == 0:
                        act.wait_ge(s_xt, 4 * k + i // 2 + 1)
                    if k + i == 0:
                        act.wait_ge(s_gc, 1)
                    src = bank[T_BANKS[k][i // 2]][:, (i % 2) * SEQ:(i % 2 + 1) * SEQ]
                    scale = 1.0 if g0 is None else g_col[:, g0 + i:g0 + i + 1]
                    A(t_hi[:, T_ORDER[k][i], :], src, ACT.Copy, scale=scale).then_inc(s_th, 1)

            def rstd_rows(n):
                act.wait_ge(s_rr, n)
                A(r_row[:, 0:SEQ], bank[7][:, 0:SEQ], ACT.Copy, scale=DH ** -0.5).then_inc(s_rc, 1)
                A(r_row[:, SEQ:], bank[7][:, 0:SEQ], ACT.Copy).then_inc(s_rc, 1)

            def ffn(f, n0):
                r0, b = R_FFN[f], f * NCH
                if f == 0:
                    split_hi(0, r0[0], 2048)
                    act.wait_ge(s_gt, 1)
                    A(g_col[:, 0:N_G], bank[7][:, 0:N_G], ACT.Copy).then_inc(s_gc, 1)
                transposed_hi(T_FFN[f], f * KT, range(0, 4))
                split_hi(1, r0[1], 2048)
                transposed_hi(T_FFN[f], f * KT, range(4, 8))
                squares(NORM_FFN[f])

                def silu(c):
                    if isinstance(c, int) and c == 0:
                        act.wait_ge(s_rs, NORM_FFN[f] + 1)
                    for t in range(NT):
                        if t == 0:
                            act.wait_ge(s_gu, c + (b + 1))
                        else:
                            act.wait_ge(s_used[1], c + (r0[1] + 1))
                        A(gate[:, t, :], bank[UP_BANKS(c)[t]][:, 0:CH], ACT.Silu, scale=rstd[:, t:t + 1]).then_inc(s_sg, 1)

                def hidden_hi(c, dst):
                    act.wait_ge(s_ht, c + (b + 1))
                    A(dst[:, 0:FT, :].rearrange("p k n -> p (k n)"), bank[2][:, :], ACT.Copy).then_inc(s_hh, 1)

                def body(c):
                    split_hi(0, c + r0[0], 2048)
                    silu(c - 1)
                    split_hi(1, c + r0[1], 2048)
                    hidden_hi(c - 1, h_hi)
                    split_hi(2, c + (r0[2] - 1), 2048)

                body(1)
                with act.Fori(2, NCH) as c:
                    body(c)
                silu(NCH - 1)
                split_hi(1, r0[1] + NCH, 2048)
                hidden_hi(NCH - 1, lt_hi)
                if n0:
                    split_hi(0, R_NORM[NORM_FFN[f] + 1][0], n0)

            for a, src in ((0, ffn_norm_g.rearrange("l s (k p) -> (l s k) p", p=P)),
                           (4 * KT, mix_norm_g.rearrange("l (k p) -> (l k) p", p=P)),
                           (G_Q, q_norm_g.rearrange("l (k p) -> (l k) p", p=P)),
                           (G_KV, kv_norm_g.rearrange("l (k p) -> (l k) p", p=P))):
                act.dma_start(g_rows[a:a + src.shape[0], :], src).then_inc(s_gr, 16)
            act.preload_act_table(ACT.Silu)
            ffn(0, 3 * LAT)

            r = R_AB
            transposed_hi(T_AB, 4 * KT, range(0, 4))
            split_hi(1, r[1], 3 * LAT)
            transposed_hi(T_AB, 4 * KT, range(4, 8))
            split_hi(2, r[2], 2 * LAT)
            split_hi(0, r[0] + 1, 3 * H_A * DH)
            squares(NORM_AB)
            split_hi(1, r[1] + 1, 3 * H_A * DH)
            split_hi(2, r[2] + 1, 2 * H_A * DH)
            act.wait_ge(s_rs, NORM_AB + 1)
            act.wait_ge(s_used[2], r[2] + 1)
            for t in range(NT):
                for i, (a, n) in enumerate(((0, RQ), (RQ, RKV))):
                    act.wait_ge(s_ss, 2 * NT) if t + i == 0 else act.wait_ge(s_lss, 2 * t + i)
                    A(junk[:, 0:n], bank[t][:, a:a + n], ACT.Square, scale=rstd[:, t:t + 1],
                      accum_out=lat_ss[:, t, i:i + 1]).then_inc(s_lss, 1)
            for t in range(NT):
                A(q_b[:, t, 8 * QD + DH:9 * QD], bank[t][:, RQ + RKV:LAT], ACT.Copy, scale=rstd[:, t:t + 1]).then_inc(s_qb, 1)
            for s, (a, b) in enumerate(KS):
                split_hi(s, r[s] + 2, (b - a) * 2 * P)
            rstd_rows(1)
            act.wait_ge(s_lt, 1)
            for i in range(3):
                A(lt_hi[:, i, :], bank[2 + i // 2][:, (i % 2) * SEQ:(i % 2 + 1) * SEQ], ACT.Copy,
                  scale=g_col[:, G_Q + i:G_Q + i + 1]).then_inc(s_lth, 1)
            act.wait_ge(s_used[2], r[2] + 2)
            act.wait_ge(s_half, 3)
            for t in range(NT):
                A(v_a[:, t, :].rearrange("p (h d) -> p h d", d=DH + 1)[:, :, 0:DH],
                  bank[4 + t][:, :].rearrange("p (h d) -> p h d", d=DH), ACT.Copy, scale=rstd[:, t:t + 1]).then_inc(s_vc, 1)
            for s, n in enumerate((H_B * QD, H_B * QD, H_B * 2 * DH)):
                split_hi(s, r[s] + 3, n)
            act.preload_act_table(ACT.Exp)
            act.wait_ge(s_used[2], r[2] + 4)
            for t in range(NT):
                for i in range(2):
                    A(v_b[:, t, i * 4 * (DH + 1):(i + 1) * 4 * (DH + 1)].rearrange("p (h d) -> p h d", d=DH + 1)[:, :, 0:DH],
                      bank[2 * t + i][:, :].rearrange("p (h d) -> p h d", d=2 * DH)[:, :, DH:2 * DH],
                      ACT.Copy).then_inc(s_vb, 1)
            split_hi(0, r[0] + 4, 3 * 2 * P)
            act.wait_ge(s_used[1], r[1] + 4)
            for t in range(NT):
                for i in range(2):
                    A(q_b[:, t, i * 4 * QD:(i + 1) * 4 * QD], bank[4 + 2 * t + i][:, 0:4 * QD], ACT.Copy,
                      scale=float(QD) ** -0.5).then_inc(s_qb, 1)

            def exps(n, e):
                act.wait_ge(s_mx, 2 * n + (e + 1))
                A(pr[e][:, 0:P], bank[e][:, 0:P], ACT.Exp, bias=nmax[:, e, 0:1])
                A(pr[e][:, P:], bank[e][:, P:3 * P], ACT.Exp, bias=nmax[:, e, 1:2]).then_inc(s_ex, 1)

            def mla_copied(j):
                act.wait_ge(s_tq, 1 + j)
                A(qk_b[0][0:QD, :], bank[5][0:QD, :], ACT.Copy).then_inc(s_qbt[0], 1)

            def probs_copied(n):
                act.wait_ge(s_pt, 2 * n + 1)
                if not (isinstance(n, int) and n == 0):
                    act.wait_ge(s_pv, n)
                A(pt[0][:, :], bank[2][:, 0:3 * P], ACT.Copy).then_inc(s_pe[0], 1)

            def ab_pair(j, n0):
                for e in range(2):
                    exps(2 * j, e)
                mla_copied(j)
                split_hi(1, j + (r[1] + 4), 3 * 2 * P)
                act.wait_ge(s_pt, 4 * j + 1)
                A(pt[0][:, :], bank[2][:, 0:3 * P], ACT.Copy).then_inc(s_pe[0], 1)
                for e in range(2):
                    exps(2 * j + 1, e)
                split_hi(2, j + (r[2] + 4), 2 * 2 * P)
                probs_copied(2 * j + 1)
                split_hi(0, j + (r[0] + 5), n0)

            act.wait_ge(s_ro, 2)
            A(q_st[:, :, :], q_b[:, :, 0:2 * QD], ACT.Copy).then_inc(s_st, 1)
            with act.Fori(0, PAIRS_A - 2) as j:
                ab_pair(j, 3 * 2 * P)
            ab_pair(PAIRS_A - 2, 3 * HALF)
            j = PAIRS_A - 1
            split_out = lambda h, s: split_hi(s, r[s] + (3 + PAIRS_A + h), (KS[s][1] - KS[s][0]) * HALF)
            for e in range(2):
                exps(2 * j, e)
            mla_copied(j)
            transposed_hi(T_AB_O, None, range(0, 2))
            probs_copied(2 * j)
            for e in range(2):
                exps(2 * j + 1, e)
            transposed_hi(T_AB_O, None, range(2, 4))
            split_out(0, 1)
            probs_copied(2 * j + 1)
            transposed_hi(T_AB_O, None, range(4, 6))
            split_out(1, 0)
            split_out(0, 2)
            transposed_hi(T_AB_O, None, range(6, 8))
            split_out(1, 1)
            act.preload_act_table(ACT.Silu)
            split_hi(0, R_FFN[1][0], 2048)
            split_out(1, 2)
            ffn(1, 2048)
            ffn(2, 3 * HALF)

            r = R_C
            transposed_hi(T_C, 5 * KT, range(0, 4))
            split_hi(1, r[1], 3 * HALF)
            transposed_hi(T_C, 5 * KT, range(4, 8))
            split_hi(2, r[2], 2 * HALF)
            squares(NORM_C)
            for s, (a, b) in enumerate(KS):
                split_hi(s, r[s] + 1, (b - a) * HALF)

            def v_half(n):
                act.wait_ge(s_used[2], r[2] + n + 1)
                for t in range(NT):
                    A(v_c[:, t, n * HALF:(n + 1) * HALF], bank[2 * n + t][:, :], ACT.Copy, scale=rstd[:, t:t + 1]).then_inc(s_vc, 1)

            act.wait_ge(s_rs, NORM_C + 1)
            v_half(0)
            split_hi(0, r[0] + 2, 3 * 2 * P)
            rstd_rows(2)
            split_hi(1, r[1] + 2, 3 * 2 * P)
            split_hi(2, r[2] + 2, 2 * 2 * P)
            v_half(1)
            act.preload_act_table_set("natural_log_exp_and_others")

            def stick_logs(j, u):
                for e in range(2):
                    act.wait_ge(s_z, 2 * j + (e + 1))
                    A(sp_abs[e][:, :], bank[Z_BANKS[u][e]][:, 0:3 * P], ACT.Abs).then_inc(s_za, 1)
                for e in range(2):
                    act.wait_ge(s_za, 2 * j + (e + 1))
                    A(sp_exp[e][:, :], sp_abs[e][:, :], ACT.Exp, scale=-1.0).then_inc(s_ze, 1)
                for e in range(2):
                    act.wait_ge(s_ze, 2 * j + (e + 1))
                    A(sp_log[e][:, :], sp_exp[e][:, :], ACT.Ln, bias=1.0).then_inc(s_zl, 1)

            def stick_hi(j):
                for e in range(2):
                    act.wait_ge(s_sp, 2 * j + (e + 1))
                    A(sp_hi[e][:, :], sp[e][:, :], ACT.Copy).then_inc(s_sh, 1)

            def stick_exp(j, u):
                for e in range(2):
                    act.wait_ge(s_cs, 2 * j + (e + 1))
                    A(pr[e][:, :], bank[Z_BANKS[u][e]][:, 0:3 * P], ACT.Exp).then_inc(s_at, 1)

            def stick_copy(j):
                act.wait_ge(s_oc, j + 1)
                A(rows[:, :, j * P:(j + 1) * P], bank[5][:, 0:SEQ].rearrange("p (t n) -> p t n", t=NT),
                  ACT.Copy).then_inc(s_oe, 1)

            for s, (a, b) in enumerate(KS):
                split_hi(s, r[s] + 3, (b - a) * 2 * P)
            stick_logs(0, 0)
            stick_hi(0)
            with act.Fori(0, PAIRS_C // 2 - 1) as i:
                for u in range(2):
                    j = i * 2 + u
                    for s, (a, b) in enumerate(KS):
                        split_hi(s, j + (r[s] + 4), (b - a) * 2 * P)
                    stick_exp(j, u)
                    stick_logs(j + 1, 1 - u)
                    stick_hi(j + 1)
            j = PAIRS_C - 2
            for s, (a, b) in enumerate(KS):
                split_hi(s, r[s] + (2 + PAIRS_C), (b - a) * HALF)
            stick_exp(j, 0)
            transposed_hi(T_C_O, None, range(0, 2))
            stick_logs(j + 1, 1)
            transposed_hi(T_C_O, None, range(2, 4))
            stick_hi(j + 1)
            transposed_hi(T_C_O, None, range(4, 6))
            stick_copy(j)
            stick_exp(j + 1, 1)
            split_hi(0, r[0] + (3 + PAIRS_C), 3 * HALF)
            stick_copy(j + 1)
            split_hi(1, r[1] + (3 + PAIRS_C), 3 * HALF)
            transposed_hi(T_C_O, None, range(6, 8))
            act.preload_act_table(ACT.Silu)
            split_hi(0, R_FFN[3][0], 2048)
            split_hi(2, r[2] + (3 + PAIRS_C), 2 * HALF)
            ffn(3, 0)

            def final_squares(p):
                h, t = PARTS(NORM_END)[p]
                act.wait_ge(s_x, 4 * (NORM_END - 1) + p + 1)
                act.wait_ge(s_ss, NT * NORM_END + p)
                A(junk[:, 0:HALF], xres[:, t, h * HALF:(h + 1) * HALF], ACT.Square,
                  accum_out=ss_h[:, t, h:h + 1]).then_inc(s_ss, 1)

            def final_rows(t):
                act.wait_ge(s_rs, NORM_END + t + 1)
                act.wait_ge(s_xg, 2 * t + 1)
                A(xres[:, t, 0:HALF], rows[:, t, 0:HALF], ACT.Copy, scale=rstd[:, t:t + 1]).then_inc(s_y0, 1)

            final_squares(0)
            final_squares(1)
            final_squares(2)
            final_squares(3)
            final_rows(0)
            final_rows(1)

        @block.vector
        def _(dve):
            V = nc.vector

            def split_lo(slot, r, n):
                dve.wait_ge(s_hi[slot], r + 1)
                V.tensor_tensor(w_lo[slot][:, 0:n], raw[slot][:, 0:n], w_hi[slot][:, 0:n].bitcast(fp32),
                                ALU.subtract).then_inc(s_lo[slot], 1)

            def residual(n, scale, parts):
                for p in parts:
                    h, t = PARTS(n)[p]
                    if n - 1 in NORM_FFN:
                        dve.wait_ge(s_acc, ACC_NORM[n - 1] + p + 1) if p < 3 else dve.wait_ge(s_used[1], R_NORM[n][1])
                    elif t == 0:
                        dve.wait_ge(s_acc, ACC_NORM[n - 1] + h + 1)
                    else:
                        dve.wait_ge(s_used[2], R_NORM[n][2] - 1 + h)
                    xs = xres[:, t, h * HALF:(h + 1) * HALF]
                    V.scalar_tensor_tensor(out=xs, in0=acc[t][h][:, :], scalar=scale, in1=xs,
                                           op0=ALU.mult, op1=ALU.add).then_inc(s_x, 1)

            def means(n):
                dve.wait_ge(s_ss, NT * n + NT)
                V.tensor_scalar(ms[:, :], ss[:, :], 1.0 / D, EPS, op0=ALU.mult, op1=ALU.add).then_inc(s_ms, 1)

            def rstd_columns(n):
                dve.wait_ge(s_rs, n + 1)
                V.tensor_copy(r_sq[:, :, :], rstd[:, :].unsqueeze(2).to_broadcast([P, NT, P])).then_inc(s_rb, 1)

            def qk_scaled(b, r, k, n):
                dve.wait_ge(s_used[2], r)
                if isinstance(n, int) and n == 0:
                    dve.wait_ge(s_rc, 2 * k)
                V.tensor_tensor(qk_t[:, :], bank[b][:, :], r_row[:, :], ALU.mult).then_inc(s_qkc, 1)

            def transposed_lo(k, g0, tiles=range(KT)):
                for i in tiles:
                    if i % 2 == 0:
                        dve.wait_ge(s_th, KT * k + i + 2)
                    src = bank[T_BANKS[k][i // 2]][:, (i % 2) * SEQ:(i % 2 + 1) * SEQ]
                    hi = t_hi[:, T_ORDER[k][i], :].bitcast(fp32)
                    if g0 is None:
                        V.tensor_tensor(t_lo[:, T_ORDER[k][i], :], src, hi, ALU.subtract).then_inc(s_tl, 1)
                    else:
                        V.scalar_tensor_tensor(out=t_lo[:, i, :], in0=src, scalar=g_col[:, g0 + i:g0 + i + 1], in1=hi,
                                               op0=ALU.mult, op1=ALU.subtract).then_inc(s_tl, 1)

            def normed(n, scale, g0, n1):
                if n:
                    residual(n, scale, (2,))
                transposed_lo(T_NORM[n], g0, range(0, 2))
                if n:
                    residual(n, scale, (3,))
                transposed_lo(T_NORM[n], g0, range(2, 4))
                split_lo(1, R_NORM[n][1], n1)
                transposed_lo(T_NORM[n], g0, range(4, 8))

            def ffn(f, scale, n0):
                r0, b, n = R_FFN[f], f * NCH, NORM_FFN[f]
                if f == 0:
                    split_lo(0, r0[0], 2048)
                elif n - 1 in NORM_FFN:
                    residual(n, scale, (0, 1))
                normed(n, scale, f * KT, 2048)
                means(NORM_FFN[f])

                def hidden(c):
                    if isinstance(c, int) and c == 0:
                        dve.wait_ge(s_rs, NORM_FFN[f] + 1)
                    for t in range(NT):
                        dve.wait_ge(s_sg, (c + b) * NT + (t + 1))
                        V.scalar_tensor_tensor(out=hid[:, t, :], in0=bank[UP_BANKS(c)[t]][:, CH:2 * CH],
                                               scalar=rstd[:, t:t + 1], in1=gate[:, t, :],
                                               op0=ALU.mult, op1=ALU.mult).then_inc(s_h, 1)

                def hidden_lo(c, hi, lo):
                    dve.wait_ge(s_hh, c + (b + 1))
                    hi, lo = (x[:, 0:FT, :].rearrange("p k n -> p (k n)") for x in (hi, lo))
                    V.tensor_tensor(lo, bank[2][:, :], hi.bitcast(fp32), ALU.subtract).then_inc(s_hl, 1)

                def body(c):
                    split_lo(0, c + r0[0], 2048)
                    hidden(c - 1)
                    split_lo(1, c + r0[1], 2048)
                    hidden_lo(c - 1, h_hi, h_lo)
                    split_lo(2, c + (r0[2] - 1), 2048)

                body(1)
                with dve.Fori(2, NCH) as c:
                    body(c)
                hidden(NCH - 1)
                split_lo(1, r0[1] + NCH, 2048)
                hidden_lo(NCH - 1, lt_hi, lt_lo)
                if n0:
                    split_lo(0, R_NORM[n + 1][0], n0)

            ffn(0, None, 3 * LAT)

            r = R_AB
            residual(NORM_AB, 0.5, (0, 1))
            normed(NORM_AB, 0.5, 4 * KT, 3 * LAT)
            split_lo(2, r[2], 2 * LAT)
            split_lo(0, r[0] + 1, 3 * H_A * DH)
            means(NORM_AB)
            split_lo(1, r[1] + 1, 3 * H_A * DH)
            split_lo(2, r[2] + 1, 2 * H_A * DH)
            rstd_columns(NORM_AB)
            dve.wait_ge(s_lss, 4)
            for i, n in enumerate((RQ, RKV)):
                V.tensor_scalar(lat_ms[:, :, i:i + 1], lat_ss[:, :, i:i + 1], 1.0 / n, EPS, op0=ALU.mult, op1=ALU.add).then_inc(s_lms, 1)
            dve.wait_ge(s_lrs, 1)
            dve.wait_ge(s_qb, 2)
            for t in range(NT):
                for i, (a, n) in enumerate(((0, RQ), (RQ, RKV))):
                    V.tensor_scalar(lat[:, t, a:a + n], bank[t][:, a:a + n], rstd[:, t:t + 1], lat_rstd[:, t, i:i + 1],
                                    op0=ALU.mult, op1=ALU.mult).then_inc(s_ln, 1)
            for s, (a, b) in enumerate(KS):
                split_lo(s, r[s] + 2, (b - a) * 2 * P)
            for i in range(3):
                dve.wait_ge(s_lth, (2, 2, 3)[i])
                V.scalar_tensor_tensor(out=lt_lo[:, i, :], in0=bank[2 + i // 2][:, (i % 2) * SEQ:(i % 2 + 1) * SEQ],
                                       scalar=g_col[:, G_Q + i:G_Q + i + 1], in1=lt_hi[:, i, :].bitcast(fp32),
                                       op0=ALU.mult, op1=ALU.subtract).then_inc(s_ltl, 1)
            for s, n in enumerate((H_B * QD, H_B * QD, H_B * 2 * DH)):
                if s == 2:
                    qk_scaled(6, r[2] + 3, 1, 0)
                split_lo(s, r[s] + 3, n)
            dve.wait_ge(s_used[2], r[2] + 4)
            for t in range(NT):
                for i in range(2):
                    dve.wait_ge(s_vb, 2 * t + i + 1)
                    V.tensor_copy(k_b[:, t, i * 4 * QD:(i + 1) * 4 * QD].rearrange("p (h d) -> p h d", d=QD)[:, :, 0:DH],
                                  bank[2 * t + i][:, :].rearrange("p (h d) -> p h d", d=2 * DH)[:, :, 0:DH]).then_inc(s_kb, 1)
            split_lo(0, r[0] + 4, 3 * 2 * P)
            dve.wait_ge(s_qb, 2 + 4)
            dve.wait_ge(s_tab, 32)
            q9 = q_b[:, :, :].rearrange("p t (h d) -> p t h d", d=QD)
            x1, x2 = q9[:, :, :, DH:DH + 16], q9[:, :, :, DH + 16:QD]
            cos, sin = (tf(n).rearrange("p (t h d) -> p t h d", t=NT, h=9) for n in ("cos", "sin"))
            for i, (u, w) in enumerate(((x1, cos), (x2, sin), (x1, sin), (x2, cos))):
                V.tensor_tensor(rot[i][:, :, :, :], u, w, ALU.mult).then_inc(s_rt, 1)
            dve.wait_ge(s_rt, 4)
            V.tensor_tensor(x1, rot[0][:, :, :, :], rot[1][:, :, :, :], ALU.subtract).then_inc(s_ro, 1)
            V.tensor_tensor(x2, rot[2][:, :, :, :], rot[3][:, :, :, :], ALU.add).then_inc(s_ro, 1)
            dve.wait_ge(s_ro, 2)
            kr = q9[:, :, 8:9, DH:QD].to_broadcast([P, NT, H_B, ROPE])
            V.tensor_copy(k_b[:, :, :].rearrange("p t (h d) -> p t h d", d=QD)[:, :, :, DH:QD], kr).then_inc(s_kr, 1)

            dve.wait_ge(s_kr, 1)
            V.tensor_copy(k_st[:, :, :], k_b[:, :, 0:2 * QD]).then_inc(s_st, 1)

            def maxima(n, e):
                dve.wait_ge(s_sc, 2 * n + (e + 1))
                V.tensor_reduce(nmax[:, e, 0:1], bank[e][:, 0:P], AX.X, ALU.max, negate=True)
                V.tensor_reduce(nmax[:, e, 1:2], bank[e][:, P:3 * P], AX.X, ALU.max, negate=True).then_inc(s_mx, 1)

            def outputs(n, col):
                dve.wait_ge(s_pv, n + 1)
                o = bank[7][:, 0:4 * (DH + 1)].rearrange("p (t h d) -> p t h d", t=NT, h=2)
                V.reciprocal(rden[:, :, :, :], o[:, :, :, DH:DH + 1]).then_inc(s_rd, 1)
                dve.wait_ge(s_rd, n + 1)
                V.tensor_tensor(rows[:, :, bass.ds(col, P)].rearrange("p t (h d) -> p t h d", h=2), o[:, :, :, 0:DH],
                                rden[:, :, :, :].to_broadcast([P, NT, 2, DH]), ALU.mult).then_inc(s_on, 1)

            def mla_copied(j):
                dve.wait_ge(s_tq, 1 + j)
                V.tensor_copy(qk_b[1][0:QD, :], bank[6][0:QD, :]).then_inc(s_qbt[1], 1)

            def probs_copied(n):
                dve.wait_ge(s_pt, 2 * n + 2)
                V.tensor_copy(pt[1][:, :], bank[3][:, 0:3 * P]).then_inc(s_pe[1], 1)

            def ab_pair(j, n0):
                for e in range(2):
                    maxima(2 * j, e)
                mla_copied(j)
                split_lo(1, j + (r[1] + 4), 3 * 2 * P)
                probs_copied(2 * j)
                for e in range(2):
                    maxima(2 * j + 1, e)
                split_lo(2, j + (r[2] + 4), 2 * 2 * P)
                outputs(2 * j, j * P)
                probs_copied(2 * j + 1)
                qk_scaled(4, j + (r[2] + 5), 1, j + 1)
                outputs(2 * j + 1, j * P + HALF)
                if n0:
                    split_lo(0, j + (r[0] + 5), n0)

            with dve.Fori(0, PAIRS_A - 2) as j:
                ab_pair(j, 3 * 2 * P)
            ab_pair(PAIRS_A - 2, 0)
            j = PAIRS_A - 1
            split_out = lambda h, s: split_lo(s, r[s] + (3 + PAIRS_A + h), (KS[s][1] - KS[s][0]) * HALF)
            for e in range(2):
                maxima(2 * j, e)
            mla_copied(j)
            split_out(0, 0)
            transposed_lo(T_AB_O, None, range(0, 2))
            probs_copied(2 * j)
            for e in range(2):
                maxima(2 * j + 1, e)
            transposed_lo(T_AB_O, None, range(2, 4))
            split_out(0, 1)
            outputs(2 * j, j * P)
            probs_copied(2 * j + 1)
            transposed_lo(T_AB_O, None, range(4, 6))
            outputs(2 * j + 1, j * P + HALF)
            split_out(1, 0)
            split_out(0, 2)
            transposed_lo(T_AB_O, None, range(6, 8))
            split_out(1, 1)
            residual(NORM_FFN[1], 1.0, (0, 1))
            split_out(1, 2)
            split_lo(0, R_FFN[1][0], 2048)
            ffn(1, 1.0, 2048)
            ffn(2, 0.5, 3 * HALF)

            r = R_C
            residual(NORM_C, 0.5, (0, 1))
            normed(NORM_C, 0.5, 5 * KT, 3 * HALF)
            split_lo(2, r[2], 2 * HALF)
            means(NORM_C)
            for s, (a, b) in enumerate(KS):
                split_lo(s, r[s] + 1, (b - a) * HALF)
            rstd_columns(NORM_C)
            for s, (a, b) in enumerate(KS):
                split_lo(s, r[s] + 2, (b - a) * 2 * P)
            for name, dst in (("neg_tri", tri_r), ("neg_one", one_r)):
                V.tensor_copy(dst[:, :], tf(name)).then_inc(s_tri, 1)
            qk_scaled(4, r[2] + 3, 2, 0)

            def stick_softplus(j, u):
                for e in range(2):
                    dve.wait_ge(s_zl, 2 * j + (e + 1))
                    V.scalar_tensor_tensor(out=sp[e][:, :], in0=bank[Z_BANKS[u][e]][:, 0:3 * P], scalar=0.0, in1=sp_log[e][:, :],
                                           op0=ALU.max, op1=ALU.add).then_inc(s_sp, 1)

            def stick_lo(j):
                for e in range(2):
                    dve.wait_ge(s_sh, 2 * j + (e + 1))
                    V.tensor_tensor(sp_lo[e][:, :], sp[e][:, :], sp_hi[e][:, :].bitcast(fp32), ALU.subtract).then_inc(s_sl, 1)

            for s, (a, b) in enumerate(KS):
                split_lo(s, r[s] + 3, (b - a) * 2 * P)
            stick_softplus(0, 0)
            stick_lo(0)
            qk_scaled(4, r[2] + 4, 2, 1)
            with dve.Fori(0, PAIRS_C // 2 - 1) as i:
                for u in range(2):
                    j = i * 2 + u
                    for s, (a, b) in enumerate(KS):
                        split_lo(s, j + (r[s] + 4), (b - a) * 2 * P)
                    stick_softplus(j + 1, 1 - u)
                    stick_lo(j + 1)
                    qk_scaled(4, j + (r[2] + 5), 2, j + 2)
                    dve.wait_ge(s_oc, j + 1)
                    V.tensor_copy(rows[:, :, bass.ds(j * P, P)],
                                  bank[5][:, 0:SEQ].rearrange("p (t n) -> p t n", t=NT)).then_inc(s_oe, 1)
            j = PAIRS_C - 2
            split_lo(0, r[0] + (2 + PAIRS_C), 3 * HALF)
            split_lo(1, r[1] + (2 + PAIRS_C), 3 * HALF)
            split_lo(2, r[2] + (2 + PAIRS_C), 2 * HALF)
            transposed_lo(T_C_O, None, range(0, 2))
            stick_softplus(j + 1, 1)
            transposed_lo(T_C_O, None, range(2, 4))
            stick_lo(j + 1)
            transposed_lo(T_C_O, None, range(4, 6))
            split_lo(0, r[0] + (3 + PAIRS_C), 3 * HALF)
            split_lo(1, r[1] + (3 + PAIRS_C), 3 * HALF)
            transposed_lo(T_C_O, None, range(6, 8))
            residual(NORM_FFN[3], 1.0, (0, 1))
            split_lo(2, r[2] + (3 + PAIRS_C), 2 * HALF)
            split_lo(0, R_FFN[3][0], 2048)
            ffn(3, 1.0, 0)

            def gained(p):
                h, t = PARTS(NORM_END)[p]
                cols = slice(h * HALF, (h + 1) * HALF)
                dve.wait_ge(s_x, 4 * (NORM_END - 1) + p + 1)
                V.tensor_tensor(rows[:, t, cols], xres[:, t, cols], g_fin[:, cols], ALU.mult).then_inc(s_xg, 1)

            def half_mean(t):
                dve.wait_ge(s_ss, NT * NORM_END + 2 * t + 1)
                V.tensor_scalar(m_0[:, t:t + 1], ss_h[:, t, 0:1], 1.0 / D, EPS, op0=ALU.mult, op1=ALU.add).then_inc(s_m0, 1)

            def mean(t):
                dve.wait_ge(s_ss, NT * NORM_END + 2 * t + 2)
                dve.wait_ge(s_m0, t + 1)
                V.tensor_scalar(ms[:, t:t + 1], ss_h[:, t, 1:2], 1.0 / D, m_0[:, t:t + 1], op0=ALU.mult, op1=ALU.add).then_inc(s_ms, 1)

            def final_rows(t):
                dve.wait_ge(s_rs, NORM_END + t + 1)
                dve.wait_ge(s_xg, 2 * t + 2)
                V.tensor_scalar(xres[:, t, HALF:], rows[:, t, HALF:], rstd[:, t:t + 1], None, op0=ALU.mult).then_inc(s_y1, 1)

            dve.wait_ge(s_gf, 16)
            residual(NORM_END, 0.5, (0,))
            gained(0)
            residual(NORM_END, 0.5, (1,))
            half_mean(0)
            gained(1)
            mean(0)
            residual(NORM_END, 0.5, (2,))
            residual(NORM_END, 0.5, (3,))
            half_mean(1)
            gained(2)
            final_rows(0)
            mean(1)
            gained(3)
            final_rows(1)

        @block.tensor
        def _(pe):
            MM = nc.tensor.matmul
            pe.sem_inc(s_on, 1)
            pe.sem_inc(s_oe, 1)

            def mm3(dst, a_hi, a_lo, b_hi, b_lo, start, stop):
                MM(dst, a_hi, b_hi, start=start, stop=False)
                MM(dst, a_hi, b_lo, start=False, stop=False)
                return MM(dst, a_lo, b_hi, start=False, stop=stop)

            def transpose_bank(k, src, t, b):
                for i in (0, 1):
                    at, c = i * SEQ + t * P, T_ORDER[k][2 * b + i] * P
                    end = nc.tensor.transpose(bank[T_BANKS[k][b]][:, at:at + P], src[:, t, c:c + P], ident)
                if t == NT - 1:
                    end.then_inc(s_xt, 1)

            def turn_residual(n, h, tiles=range(NT)):
                if 0 < n < NORM_END:
                    for t in tiles:
                        pe.wait_ge(s_x, 4 * (n - 1) + 2 * h + t + 1)
                        for b in (2 * h, 2 * h + 1):
                            transpose_bank(T_NORM[n], xres, t, b)

            def rstd_transposed(k):
                pe.wait_ge(s_rb, k)
                for t in range(NT):
                    end = MM(bank[7][:, t * P:(t + 1) * P], r_sq[:, t, :], ident, start=t == 0, stop=t == 1,
                             skip_group_check=True)
                end.then_inc(s_rr, 1)

            T = (t_hi, t_lo)

            def by_slot(slot, r, tiles, lhs, n, dst, first, last, tile_done=None, T_k=None, between=None):
                pe.wait_ge(s_lo[slot], r + 1)
                for t in range(NT):
                    outs = dst(t)
                    for i, k in enumerate(tiles):
                        if t == 0 and T_k is not None:
                            pe.wait_ge(s_tl, KT * T_k + T_ORDER[T_k].index(k) + 1)
                        hi, lo = (x[:, k, t * P:(t + 1) * P] for x in lhs)
                        for m, o in enumerate(outs):
                            c = (i * len(outs) + m) * n
                            end = mm3(o, hi, lo, w_hi[slot][:, c:c + n], w_lo[slot][:, c:c + n],
                                      first and i == 0, last and i == len(tiles) - 1)
                    if t == 0 and tile_done is not None:
                        end.then_inc(tile_done, 1)
                    if t == 0 and between is not None:
                        between()
                end.then_inc(s_used[slot], 1)

            def block_round(R, r, n, dst, k=None, between=None):
                for s, (a, b) in enumerate(KS):
                    by_slot(s, R[s] + r, range(a, b), T, n, dst, s == 0, s == 2, T_k=k, between=between if s == 0 else None)

            def project_part(R, r, k, h, slot, between=None):
                a, b = KS[slot]
                by_slot(slot, R[slot] + r + h, range(a, b), T, HALF, lambda t: [acc[t][h][:, :]], slot == 0, slot == 2,
                        s_acc if slot == 2 else None, T_k=k, between=between)

            def project_qk(slot, r, bk):
                a, b = KS[slot]
                pe.wait_ge(s_lo[slot], r + 1)
                for k in range(a, b):
                    for i in range(2):
                        c = ((k - a) * 2 + i) * P
                        dst = bk[:, i * SEQ:(i + 1) * SEQ]
                        hi, lo = w_hi[slot][:, c:c + P], w_lo[slot][:, c:c + P]
                        MM(dst, hi, t_hi[:, k, :], start=k == 0 and i == 0, stop=False, skip_group_check=True)
                        MM(dst, hi, t_lo[:, k, :], start=False, stop=False, skip_group_check=True)
                        end = MM(dst, lo, t_hi[:, k, :], start=False, stop=k == KT - 1 and i == 1, skip_group_check=True)
                end.then_inc(s_used[slot], 1)

            def ffn(f):
                r0, b = R_FFN[f], f * NCH
                n = NORM_FFN[f]

                def up(c, slot, k=None, between=None):
                    by_slot(slot, c + r0[slot], range(4 * slot, 4 * slot + 4), T, 2 * CH, lambda t: [bank[UP_BANKS(c)[t]][:, :]],
                            slot == 0, slot == 1, s_gu if slot == 1 else None, T_k=k, between=between)

                def turn(c):
                    for t in range(NT):
                        pe.wait_ge(s_h, (c + b) * NT + (t + 1))
                        for k in range(FT):
                            end = nc.tensor.transpose(bank[2][:, k * SEQ + t * P:k * SEQ + (t + 1) * P],
                                                      hid[:, t, k * P:(k + 1) * P], ident)
                    end.then_inc(s_ht, 1)

                def down_part(hidden, slot, t, h, first, last):
                    for k in range(FT):
                        hi, lo = (x[:, k, t * P:(t + 1) * P] for x in hidden)
                        at = slice((k * 2 + h) * HALF, (k * 2 + h + 1) * HALF)
                        end = mm3(acc[t][h][:, :], hi, lo, w_hi[slot][:, at], w_lo[slot][:, at],
                                  first and k == 0, last and k == FT - 1)
                    return end

                def down(c, first, turn_next=False):
                    pe.wait_ge(s_hl, c + (b + 1))
                    pe.wait_ge(s_lo[2], c + (r0[2] + 1))
                    for t in range(NT):
                        for h in range(2):
                            end = down_part((h_hi, h_lo), 2, t, h, first, False)
                        if t == 0 and turn_next:
                            turn(c + 1)
                    end.then_inc(s_used[2], 1)

                def last_down(c):
                    pe.wait_ge(s_hl, c + (b + 1))
                    pe.wait_ge(s_lo[1], r0[1] + NCH + 1)
                    for p in range(4):
                        h, t = PARTS(n + 1)[p]
                        if p == 3:
                            turn_residual(n + 1, 0)
                        down_part((lt_hi, lt_lo), 1, t, h, False, True).then_inc(s_acc if p < 3 else s_used[1], 1)
                    turn_residual(n + 1, 1, (0,))

                up(0, 0, T_FFN[f], lambda: turn_residual(n, 1, (1,)))
                up(0, 1, T_FFN[f])
                up(1, 0)
                turn(0)
                up(1, 1)
                down(0, True)
                with pe.Fori(2, NCH - 1) as c:
                    turn(c - 1)
                    up(c, 0)
                    up(c, 1)
                    down(c - 1, False)
                turn(NCH - 2)
                up(NCH - 1, 0)
                up(NCH - 1, 1)
                down(NCH - 2, False, turn_next=True)
                last_down(NCH - 1)

            pe.wait_ge(s_half, 2)
            for i in range(WARM_UP):
                MM(bank[6][:, :], v_a[:, 0, 0:P], v_a[:, 0, 0:HALF], start=True, stop=True)
            pe.wait_ge(s_id, 16)
            pe.wait_ge(s_gr, 4 * 16)
            nc.tensor.transpose(bank[7][:, 0:N_G], g_rows[0:N_G, :], ident[0:N_G, 0:N_G]).then_inc(s_gt, 1)
            for t in range(NT):
                pe.wait_ge(s_in[t], 16)
                for b in range(KT // 2):
                    transpose_bank(T_FFN[0], xres, t, b)
            ffn(0)

            r = R_AB
            block_round(r, 0, LAT, lambda t: [bank[t][:, 0:LAT]], T_AB, lambda: turn_residual(NORM_AB, 1, (1,)))
            block_round(r, 1, H_A * DH, lambda t: [bank[4 + t][:, :]])
            rstd_transposed(1)
            pe.wait_ge(s_ln, 4)
            for t in range(NT):
                for i in range(3):
                    end = nc.tensor.transpose(bank[2 + i // 2][:, (i % 2) * SEQ + t * P:(i % 2) * SEQ + (t + 1) * P],
                                              lat[:, t, i * P:(i + 1) * P], ident)
            end.then_inc(s_lt, 1)
            for s in range(3):
                project_qk(s, r[s] + 2, bank[6])
            LT = (lt_hi, lt_lo)
            pe.wait_ge(s_vc, NT)
            pe.wait_ge(s_ltl, 3)

            def q_banks(t):
                if t == 1:
                    pe.wait_ge(s_qkc, 1)
                return [bank[4 + 2 * t + i][:, 0:4 * QD] for i in range(2)]

            by_slot(0, r[0] + 3, [0], LT, 4 * QD, q_banks, True, False)
            by_slot(2, r[2] + 3, [2], LT, 4 * 2 * DH, lambda t: [bank[2 * t + i][:, :] for i in range(2)], True, True)
            by_slot(1, r[1] + 3, [1], LT, 4 * QD, q_banks, False, True)

            pe.wait_ge(s_kb, 4)

            def scores_a(j):
                pe.wait_ge(s_qkc, j + 1)
                for e in range(2):
                    q, k = (qk_t[e * DH:(e + 1) * DH, i * SEQ:(i + 1) * SEQ] for i in range(2))
                    MM(bank[e][:, 0:3 * P], tabb[:, bass.ds(j * (2 * P) + (BC["slopes"][0] + e * P), P)], tb("dist"), start=True, stop=False, skip_group_check=True)
                    MM(bank[e][:, 0:P], q[:, 0:P], k[:, 0:P], start=False, stop=False, skip_group_check=True)
                    MM(bank[e][:, P:3 * P], q[:, P:SEQ], k, start=False, stop=True, skip_group_check=True).then_inc(s_sc, 1)

            def scores_b(j):
                for e in range(2):
                    pe.wait_ge(s_qbt[e], j + 1)
                    q, k = (qk_b[e][0:QD, i * SEQ:(i + 1) * SEQ] for i in range(2))
                    MM(bank[e][:, 0:3 * P], tb("identb"), tb("causal"), start=True, stop=False, skip_group_check=True)
                    MM(bank[e][:, 0:P], q[:, 0:P], k[:, 0:P], start=False, stop=False, skip_group_check=True)
                    MM(bank[e][:, P:3 * P], q[:, P:SEQ], k, start=False, stop=True, skip_group_check=True).then_inc(s_sc, 1)

            def turn_probs(src, e):
                for i in range(3):
                    end = nc.tensor.transpose(bank[2 + e][:, i * P:(i + 1) * P], src[e][:, i * P:(i + 1) * P], ident)
                end.then_inc(s_pt, 1)

            def weigh(n, v, col):
                pe.wait_ge(s_pe[0], n + 1)
                pe.wait_ge(s_pe[1], n + 1)
                pe.wait_ge(s_on, n + 1)
                for t in range(NT):
                    for e in range(2):
                        w = DH + 1
                        dst = bank[7][:, (2 * t + e) * w:(2 * t + e + 1) * w]
                        for i in range(t + 1):
                            end = MM(dst, pt[e][:, (t + i) * P:(t + i + 1) * P], v[:, i, bass.ds(col + e * w, w)],
                                     start=t == 0 and e == 0, stop=t == 1 and e == 1 and i == 1, skip_group_check=True)
                end.then_inc(s_pv, 1)

            def turn_mla(j):
                pe.wait_ge(s_st, 2 * j + 2)
                for e in range(2):
                    for i, st in enumerate((q_st, k_st)):
                        for t in range(NT):
                            end = nc.tensor.transpose(bank[5 + e][0:QD, i * SEQ + t * P:i * SEQ + (t + 1) * P],
                                                      st[:, t, e * QD:(e + 1) * QD], ident)
                end.then_inc(s_tq, 1)

            def turn_counted(j):
                for e in range(2):
                    pe.wait_ge(s_cn, 2 * j + (e + 1))
                    turn_probs(pc, e)

            def turn_mla_probs(j):
                for e in range(2):
                    pe.wait_ge(s_ex, 4 * j + (e + 3))
                    turn_probs(pr, e)

            def ab_pair(j):
                scores_a(j)
                project_qk(0, j + (r[0] + 4), bank[4])
                turn_mla(j)
                turn_counted(j)
                scores_b(j)
                project_qk(1, j + (r[1] + 4), bank[4])
                weigh(2 * j, v_a, j * (2 * (DH + 1)))
                turn_mla_probs(j)
                project_qk(2, j + (r[2] + 4), bank[4])
                weigh(2 * j + 1, v_b, j * (2 * (DH + 1)))

            pe.wait_ge(s_qb, 2 + 1)
            with pe.Fori(0, PAIRS_A - 1) as j:
                ab_pair(j)

            def turn_outputs(b):
                for t in range(NT):
                    transpose_bank(T_AB_O, rows, t, b)

            j = PAIRS_A - 1
            part = lambda h, s, between=None: project_part(R_AB, 3 + PAIRS_A, T_AB_O, h, s, between)
            scores_a(j)
            turn_mla(j)
            pe.wait_ge(s_on, 1 + 2 * j)
            turn_outputs(0)
            turn_counted(j)
            scores_b(j)
            turn_outputs(1)
            weigh(2 * j, v_a, j * (2 * (DH + 1)))
            pe.wait_ge(s_tl, KT * T_AB_O + 3)
            part(0, 0)
            turn_mla_probs(j)
            turn_outputs(2)
            weigh(2 * j + 1, v_b, j * (2 * (DH + 1)))

            def part_of_slot_1(tiles, there):
                pe.wait_ge(s_tl, KT * T_AB_O + there)
                for t in range(NT):
                    for k in tiles:
                        hi, lo = (x[:, k, t * P:(t + 1) * P] for x in T)
                        at = slice((k - KS[1][0]) * HALF, (k - KS[1][0] + 1) * HALF)
                        end = mm3(acc[t][0][:, :], hi, lo, w_hi[1][:, at], w_lo[1][:, at], False, False)
                return end

            pe.wait_ge(s_lo[1], r[1] + (4 + PAIRS_A))
            part_of_slot_1((4, 5), KT - 2)
            pe.wait_ge(s_on, 1 + 2 * PAIRS_A)
            turn_outputs(3)
            part(1, 0, lambda: part_of_slot_1((3,), KT - 1).then_inc(s_used[1], 1))
            part(0, 2)
            part(1, 1)
            turn_residual(NORM_AB + 1, 0)
            part(1, 2)
            turn_residual(NORM_AB + 1, 1, (0,))
            ffn(1)
            ffn(2)

            r = R_C
            block_round(r, 0, HALF, lambda t: [bank[t][:, :]], T_C, lambda: turn_residual(NORM_C, 1, (1,)))
            for s, (a, b) in enumerate(KS):
                by_slot(s, r[s] + 1, range(a, b), T, HALF, lambda t: [bank[2 + t][:, :]], s == 0, s == 2)
                if s == 0:
                    rstd_transposed(2)
            for s in range(3):
                project_qk(s, r[s] + 2, bank[4])
            pe.wait_ge(s_vc, 3 * NT)
            pe.wait_ge(s_tri, 2)

            def stick_z(j, u):
                pe.wait_ge(s_qkc, j + (PAIRS_A + 1))
                for e in range(2):
                    q, k = (qk_t[e * DH:(e + 1) * DH, i * SEQ:(i + 1) * SEQ] for i in range(2))
                    z = bank[Z_BANKS[u][e]]
                    MM(z[:, 0:3 * P], tb("identb"), tb("strict"), start=True, stop=False, skip_group_check=True)
                    MM(z[:, 0:SEQ], k[:, 0:P], q, start=False, stop=False, skip_group_check=True)
                    MM(z[:, SEQ:3 * P], k[:, P:SEQ], q[:, P:SEQ], start=False, stop=True,
                       skip_group_check=True).then_inc(s_z, 1)

            def stick_sums(j, u):
                for e in range(2):
                    pe.wait_ge(s_sl, 2 * j + (e + 1))
                    z = bank[Z_BANKS[u][e]]
                    for part in (sp_hi[e], sp_lo[e]):
                        MM(z[:, 0:3 * P], tri_r[:, :], part[:, :], start=False, stop=False, skip_group_check=True)
                    for part in (sp_hi[e], sp_lo[e]):
                        end = MM(z[:, P:SEQ], one_r[:, :], part[:, SEQ:], start=False, stop=part is sp_lo[e],
                                 skip_group_check=True)
                    end.then_inc(s_cs, 1)

            def stick_weigh(j):
                pe.wait_ge(s_oe, j + 1)
                for e in range(2):
                    pe.wait_ge(s_at, 2 * j + (e + 1))
                    for t in range(NT):
                        dst = bank[5][:, (2 * t + e) * DH:(2 * t + e + 1) * DH]
                        for i in range(t + 1):
                            c = (t + i) * P
                            end = MM(dst, pr[e][:, c:c + P], v_c[:, i, bass.ds(j * P + e * DH, DH)],
                                     start=t == 0 and e == 0, stop=e == 1 and t == 1 and i == 1, skip_group_check=True)
                end.then_inc(s_oc, 1)

            stick_z(0, 0)
            for s in range(3):
                project_qk(s, r[s] + 3, bank[4])
            with pe.Fori(0, PAIRS_C // 2 - 1) as i:
                for u in range(2):
                    j = i * 2 + u
                    stick_sums(j, u)
                    stick_z(j + 1, 1 - u)
                    for s in range(3):
                        project_qk(s, j + (r[s] + 4), bank[4])
                    stick_weigh(j)
            def outputs_turned(bs, pairs):
                pe.wait_ge(s_oe, 1 + pairs)
                for b in bs:
                    for t in range(NT):
                        transpose_bank(T_C_O, rows, t, b)

            j = PAIRS_C - 2
            stick_sums(j, 0)
            outputs_turned((0,), 2)
            stick_z(j + 1, 1)
            pe.wait_ge(s_at, 2 * j + 2)
            outputs_turned((1, 2), 6)
            stick_weigh(j)
            part = lambda h, s, between=None: project_part(R_C, 2 + PAIRS_C, T_C_O, h, s, between)
            part(0, 0)
            stick_sums(j + 1, 1)
            part(0, 1, lambda: stick_weigh(j + 1))
            outputs_turned((3,), 8)
            part(1, 0)
            part(0, 2)
            part(1, 1)
            turn_residual(NORM_C + 1, 0)
            part(1, 2)
            turn_residual(NORM_C + 1, 1, (0,))
            ffn(3)


_INS = ["x", "ffn_norm_g", "mix_norm_g", "ffn_w_gate", "ffn_w_up", "ffn_w_down", "ab_w_in", "mla_q_norm_g",
        "mla_w_uq", "mla_kv_norm_g", "mla_w_ukv", "ab_w_out", "sb_w_in", "sb_w_out", "final_norm_g"]


def tables(np):
    f, nf, b, nb = layout(1024, 2816, 256)
    tf, tb = np.zeros((P, nf), np.float32), np.zeros((P, nb), np.float32)
    row, col = np.arange(P)[:, None], np.arange(P)[None, :]

    def put(t, at, name, values):
        t[:, at[name][0]:at[name][1]] = np.asarray(values, np.float32).reshape(P, -1)

    put(tf, f, "ident", row == col)
    put(tf, f, "neg_tri", -1.0 * (row >= col))
    put(tf, f, "neg_one", -np.ones((P, P)))
    dist = np.concatenate([row - col, row - col + P, row - col], axis=1)
    count = (dist >= 0) * ((dist <= 128) * 1 + (dist % 4 == 0) + (dist % 16 == 0))
    put(tf, f, "count", count)
    put(tb, b, "dist", np.where(count > 0, -dist, NEG))
    put(tb, b, "causal", np.where(dist >= 0, 0.0, NEG))
    put(tb, b, "identb", row == col)
    put(tb, b, "slopes", np.concatenate([2.0 ** -(h + 1) * (row == col) for h in range(8)], axis=1))
    strict = np.where(row < col, 0.0, NEG)
    put(tb, b, "strict", np.concatenate([strict, np.zeros((P, P)), strict], axis=1))
    inv = np.float32(10000.0) ** (-np.arange(0, 32, 2, dtype=np.float32) / np.float32(32))
    ang = np.arange(256, dtype=np.float32)[:, None] * inv[None, :].astype(np.float32)
    for name, fn in (("cos", np.cos), ("sin", np.sin)):
        put(tf, f, name, np.repeat(fn(ang).reshape(2, P, 1, 16).transpose(1, 0, 2, 3), 9, axis=2))
    return tf, (tb.view(np.uint32) >> 16).astype(np.uint16)


def kernel(**inputs):
    import numpy as np
    import concourse.bacc as bacc
    from concourse.bass_utils import run_bass_kernel_spmd

    nc = bacc.Bacc("TRN2", target_bir_lowering=False, num_devices=1)
    arrays, args = {}, []
    table_f, table_b = tables(np)
    for name, a in [(n, inputs[n]) for n in _INS] + [("table_f", table_f), ("table_b", table_b)]:
        a = np.ascontiguousarray(a)
        arrays[f"in_{name}_dram"] = a
        args.append(nc.dram_tensor(f"in_{name}_dram", a.shape, mybir.dt.from_np(a.dtype), kind="ExternalInput").ap())
    shape = tuple(inputs["x"].shape)
    out = nc.dram_tensor("out_0_dram", shape, mybir.dt.float32, kind="ExternalOutput").ap()
    trunk_kernel(nc, *args, out)
    r = run_bass_kernel_spmd(nc, [arrays], core_ids=[0])
    return r.results[0]["out_0_dram"]
```
